# Optimizing a Trainium2 kernel written in Bass

```python
import math
import jax
import jax.numpy as jnp
from jax import lax
import numpy as np

D_MODEL = 1024
BATCH = 1
SEQ = 512
DEPTH = 2
DEC_BATCH = 8
DEC_SEQ = 1
PAST_LEN = 512
PAGE_SIZE = 128

DEPTH_A = DEPTH // 2
DEPTH_B = DEPTH - DEPTH_A
A_HEAD = 64
A_HEADS = D_MODEL // A_HEAD
LORA_DECAY = 64
LORA_AAA = 64
LORA_MV = 32
LORA_GATE = 160
LNX_EPS = 64e-5
WINDOWS = (128, 512, 2048)
DILATIONS = (1, 4, 16)
N_GROUPS_B = len(WINDOWS)
B_HEAD = 64
B_HEADS_PER_GROUP = D_MODEL // B_HEAD
B_KV_HEADS = 4
B_REP = B_HEADS_PER_GROUP // B_KV_HEADS
QBLOCK = 128
N_BUCKETS = 32
MAX_DISTANCE = 2048
MOE_GROUPS = 4
MOE_EXPERTS_PER_GROUP = 4
MOE_EXPERTS = MOE_GROUPS * MOE_EXPERTS_PER_GROUP
MOE_TOP_K = 2
MOE_HIDDEN = 512
ALPHA = (2.0 * DEPTH) ** 0.25
BETA = (8.0 * DEPTH) ** -0.25
LN_EPS = 1e-5

kernel_name = 'yoco_rwkv7_dilated_hmoe_step'

def layer_norm(x, g, b):
    xf = x.astype(jnp.float32)
    mu = jnp.mean(xf, axis=-1, keepdims=True)
    var = jnp.mean(jnp.square(xf - mu), axis=-1, keepdims=True)
    return ((xf - mu) * lax.rsqrt(var + LN_EPS) * g + b).astype(x.dtype)

def rwkv7_time_mix(x, shift_prev, s0, v_first, p, l):
    bq, t, d = x.shape
    heads = lambda z: z.reshape(bq, t, A_HEADS, A_HEAD)
    x_prev = jnp.concatenate([shift_prev[:, None, :], x[:, :-1]], axis=1)
    xm = x[None] + (x_prev - x)[None] * p['a_mu'][l][:, None, None, :]
    xr, xw, xk, xv, xa, xg = xm
    r, k, v = jnp.einsum('cbtd,cde->cbte', jnp.stack([xr, xk, xv]), p['a_w_rkv'][l])
    w_log = -jax.nn.softplus(-(p['a_w0'][l] + jnp.tanh(xw @ p['a_w1'][l]) @ p['a_w2'][l]).astype(jnp.float32)) - 0.5
    decay = jnp.exp(-jnp.exp(w_log)).astype(x.dtype)
    a = jax.nn.sigmoid(p['a_a0'][l] + (xa @ p['a_a1'][l]) @ p['a_a2'][l])
    g = jax.nn.sigmoid(xg @ p['a_g1'][l]) @ p['a_g2'][l]
    if l == 0:
        v_first = v
    else:
        v = v + (v_first - v) * jax.nn.sigmoid(p['a_v0'][l - 1] + (xv @ p['a_v1'][l - 1]) @ p['a_v2'][l - 1])
    kk = heads(k * p['a_k_k'][l]).astype(jnp.float32)
    kk = (kk * lax.rsqrt(jnp.maximum(jnp.sum(kk * kk, axis=-1, keepdims=True), 1e-24))).astype(x.dtype)
    k = k * (1.0 + (a - 1.0) * p['a_k_a'][l])
    rh, kh, vh, ah, wh = heads(r), heads(k), heads(v), heads(a), heads(decay)
    xs = tuple(jnp.moveaxis(z, 1, 0) for z in (rh, wh, kh, vh, -kk, kk * ah))

    def step(s, inp):
        r_t, w_t, k_t, v_t, a_t, b_t = inp
        sa = jnp.einsum('bhij,bhj->bhi', s, a_t)
        s = s * w_t[:, :, None, :] + sa[..., None] * b_t[:, :, None, :] + v_t[..., None] * k_t[:, :, None, :]
        return s, jnp.einsum('bhij,bhj->bhi', s, r_t)

    s_fin, y = lax.scan(step, s0, xs)
    y = jnp.moveaxis(y, 0, 1).astype(jnp.float32)
    mu = jnp.mean(y, axis=-1, keepdims=True)
    var = jnp.mean(jnp.square(y - mu), axis=-1, keepdims=True)
    yn = ((y - mu) * lax.rsqrt(var + LNX_EPS)).reshape(bq, t, d) * p['a_lnx_g'][l] + p['a_lnx_b'][l]
    bonus = (jnp.sum(rh * kh * p['a_r_k'][l], axis=-1, keepdims=True) * vh).reshape(bq, t, d)
    out = ((yn.astype(x.dtype) + bonus) * g) @ p['a_w_o'][l]
    return out, x[:, -1], s_fin, v_first

def t5_bucket(dist):
    exact = N_BUCKETS // 2
    d_f = jnp.maximum(dist, 1).astype(jnp.float32)
    large = exact + (jnp.log(d_f / exact) / math.log(MAX_DISTANCE / exact) * (N_BUCKETS - exact)).astype(jnp.int32)
    large = jnp.minimum(large, N_BUCKETS - 1)
    return jnp.where(dist < exact, dist, large)

def dilated_group_attention(q, kv, q_pos, offs, bias):
    bq, t, hg, dh = q.shape
    qb = QBLOCK if t % QBLOCK == 0 else t
    nb = t // qb
    q_blocks = jnp.moveaxis(q.reshape(bq, nb, qb, B_KV_HEADS, B_REP, dh), 1, 0)
    pos_blocks = q_pos.reshape(nb, qb)
    bias = bias.reshape(B_KV_HEADS, B_REP, -1).astype(jnp.float32)
    scale = dh ** -0.5

    def attend_block(args):
        qblk, pos = args
        idx = pos[:, None] - offs[None, :]
        valid = idx >= 0
        kvg = kv[:, jnp.maximum(idx, 0)]
        s = jnp.einsum('bqgrd,bqkgd->bqgrk', qblk, kvg[:, :, :, 0]).astype(jnp.float32) * scale + bias
        s = jnp.where(valid[None, :, None, None, :], s, -jnp.inf)
        m = jnp.max(s, axis=-1, keepdims=True)
        pe = jnp.exp(s - m)
        z = jnp.sum(pe, axis=-1, keepdims=True)
        o = jnp.einsum('bqgrk,bqkgd->bqgrd', (pe / z).astype(kvg.dtype), kvg[:, :, :, 1])
        return o, (m + jnp.log(z))[..., 0]

    o, lse = lax.map(attend_block, (q_blocks, pos_blocks))
    o = jnp.moveaxis(o, 0, 1).reshape(bq, t, hg, dh)
    lse = jnp.moveaxis(lse, 0, 1).reshape(bq, t, hg)
    return o, lse

def dilated_mixture_attention(x, kv_ext, rel_bias, w_q, w_o):
    bq, t, _ = x.shape
    q = (x @ w_q).reshape(bq, t, N_GROUPS_B, B_HEADS_PER_GROUP, B_HEAD)
    outs, lses = [], []
    for g in range(N_GROUPS_B):
        n_keys = WINDOWS[g] // DILATIONS[g] + 1
        offs = DILATIONS[g] * jnp.arange(n_keys, dtype=jnp.int32)
        bias = rel_bias[t5_bucket(offs), g * B_HEADS_PER_GROUP:(g + 1) * B_HEADS_PER_GROUP].T
        q_pos = kv_ext[g].shape[1] - t + jnp.arange(t, dtype=jnp.int32)
        o, lse = dilated_group_attention(q[:, :, g], kv_ext[g], q_pos, offs, bias)
        outs.append(o)
        lses.append(lse)
    wgt = jax.nn.softmax(jnp.stack(lses), axis=0)
    o = jnp.sum(wgt[..., None].astype(x.dtype) * jnp.stack(outs), axis=0)
    return o.reshape(bq, t, B_HEADS_PER_GROUP * B_HEAD) @ w_o

def hier_moe(x, w_gc, b_gc, w_gf, b_gf, w_gate, w_up, w_down):
    shp = x.shape
    xt = x.reshape(-1, D_MODEL)
    n = xt.shape[0]
    pc = jax.nn.softmax((xt @ w_gc + b_gc).astype(jnp.float32), axis=-1)
    pg, gi = lax.top_k(pc, 1)
    lf = jnp.einsum('td,dge->tge', xt, w_gf) + b_gf
    lf = jnp.take_along_axis(lf, jnp.broadcast_to(gi[:, :, None], (n, 1, MOE_EXPERTS_PER_GROUP)), axis=1)[:, 0]
    pf = jax.nn.softmax(lf.astype(jnp.float32), axis=-1)
    pe, ei = lax.top_k(pf, MOE_TOP_K)
    pe = pe / jnp.sum(pe, axis=-1, keepdims=True)
    expert_id = gi * MOE_EXPERTS_PER_GROUP + ei
    comb = jnp.sum((pg * pe)[..., None] * jax.nn.one_hot(expert_id, MOE_EXPERTS, dtype=jnp.float32), axis=1).astype(x.dtype)
    y = jnp.zeros_like(xt)
    for e in range(MOE_EXPERTS):
        h = jax.nn.silu(xt @ w_gate[e]) * (xt @ w_up[e])
        y = y + comb[:, e:e + 1] * (h @ w_down[e])
    return y.reshape(shp)

def trunk(x, shift_init, wkv_init, kv_past, p):
    shifts, states = [], []
    v_first = None
    kv_new, kv_ext = None, None
    for layer in range(DEPTH):
        if layer < DEPTH_A:
            h, sh, s_fin, v_first = rwkv7_time_mix(x, shift_init[layer], wkv_init[layer], v_first, p, layer)
            shifts.append(sh)
            states.append(s_fin)
        else:
            lb = layer - DEPTH_A
            h = dilated_mixture_attention(x, kv_ext, p['rel_bias'], p['b_w_q'][lb], p['b_w_o'][lb])
        x = layer_norm(ALPHA * x + h, p['ln_g'][layer, 0], p['ln_b'][layer, 0])
        m = hier_moe(x, p['moe_w_gc'][layer], p['moe_b_gc'][layer], p['moe_w_gf'][layer], p['moe_b_gf'][layer],
                     p['moe_w_gate'][layer], p['moe_w_up'][layer], p['moe_w_down'][layer])
        x = layer_norm(ALPHA * x + m, p['ln_g'][layer, 1], p['ln_b'][layer, 1])
        if layer == DEPTH_A - 1:
            kv_new = jnp.einsum('btd,dgsnh->btgsnh', x, p['b_w_kv'])
            kv_ext = tuple(jnp.concatenate([kv_past[g], kv_new[:, :, g]], axis=1) for g in range(N_GROUPS_B))
    return x, jnp.stack(states), jnp.stack(shifts), kv_new

def setup_inputs(seed: int = 0) -> dict:
    key = jax.random.key(seed)
    keys = iter(jax.random.split(key, 48))

    def nrm(shape, scale):
        return scale * jax.random.normal(next(keys), shape, jnp.float32)

    def uni(shape, lo, hi):
        return jax.random.uniform(next(keys), shape, jnp.float32, lo, hi)

    d, da, db = D_MODEL, DEPTH_A, DEPTH_B
    hb = N_GROUPS_B * B_HEADS_PER_GROUP
    kv_rows = [min(w, PAST_LEN) for w in WINDOWS]
    return {
        'x_prompt': nrm((BATCH, SEQ, d), 1.0),
        'x_sample': nrm((DEC_BATCH, DEC_SEQ, d), 1.0),
        'state_a_wkv': nrm((da, DEC_BATCH, A_HEADS, A_HEAD, A_HEAD), 0.5),
        'state_a_shift': nrm((da, DEC_BATCH, d), 1.0),
        'cache_kv_g0': nrm((DEC_BATCH, kv_rows[0], 2, B_KV_HEADS, B_HEAD), 1.0),
        'cache_kv_g1': nrm((DEC_BATCH, kv_rows[1], 2, B_KV_HEADS, B_HEAD), 1.0),
        'cache_kv_g2': nrm((DEC_BATCH, kv_rows[2], 2, B_KV_HEADS, B_HEAD), 1.0),
        'ln_g': 1.0 + nrm((DEPTH, 2, d), 0.05),
        'ln_b': nrm((DEPTH, 2, d), 0.02),
        'a_mu': uni((da, 6, d), 0.0, 1.0),
        'a_w_rkv': nrm((da, 3, d, d), d ** -0.5),
        'a_w0': uni((da, d), -6.0, 1.0),
        'a_w1': nrm((da, d, LORA_DECAY), d ** -0.5),
        'a_w2': nrm((da, LORA_DECAY, d), 0.5 * LORA_DECAY ** -0.5),
        'a_a0': nrm((da, d), 0.1),
        'a_a1': nrm((da, d, LORA_AAA), d ** -0.5),
        'a_a2': nrm((da, LORA_AAA, d), 0.5 * LORA_AAA ** -0.5),
        'a_v0': nrm((da - 1, d), 0.1),
        'a_v1': nrm((da - 1, d, LORA_MV), d ** -0.5),
        'a_v2': nrm((da - 1, LORA_MV, d), 0.5 * LORA_MV ** -0.5),
        'a_g1': nrm((da, d, LORA_GATE), d ** -0.5),
        'a_g2': nrm((da, LORA_GATE, d), LORA_GATE ** -0.5),
        'a_k_k': 0.85 + nrm((da, d), 0.05),
        'a_k_a': 1.0 + nrm((da, d), 0.05),
        'a_r_k': nrm((da, A_HEADS, A_HEAD), 0.1),
        'a_lnx_g': 1.0 + nrm((da, d), 0.05),
        'a_lnx_b': nrm((da, d), 0.02),
        'a_w_o': nrm((da, d, d), BETA * d ** -0.5),
        'b_w_kv': nrm((d, N_GROUPS_B, 2, B_KV_HEADS, B_HEAD), d ** -0.5),
        'b_w_q': nrm((db, d, hb * B_HEAD), d ** -0.5),
        'b_w_o': nrm((db, B_HEADS_PER_GROUP * B_HEAD, d), BETA * (B_HEADS_PER_GROUP * B_HEAD) ** -0.5),
        'rel_bias': nrm((N_BUCKETS, hb), 0.5),
        'moe_w_gc': nrm((DEPTH, d, MOE_GROUPS), d ** -0.5),
        'moe_b_gc': nrm((DEPTH, MOE_GROUPS), 0.01),
        'moe_w_gf': nrm((DEPTH, d, MOE_GROUPS, MOE_EXPERTS_PER_GROUP), d ** -0.5),
        'moe_b_gf': nrm((DEPTH, MOE_GROUPS, MOE_EXPERTS_PER_GROUP), 0.01),
        'moe_w_gate': nrm((DEPTH, MOE_EXPERTS, d, MOE_HIDDEN), d ** -0.5),
        'moe_w_up': nrm((DEPTH, MOE_EXPERTS, d, MOE_HIDDEN), d ** -0.5),
        'moe_w_down': nrm((DEPTH, MOE_EXPERTS, MOE_HIDDEN, d), BETA * MOE_HIDDEN ** -0.5),
    }

def reference(x_prompt, x_sample, state_a_wkv, state_a_shift, cache_kv_g0, cache_kv_g1, cache_kv_g2,
              ln_g, ln_b, a_mu, a_w_rkv, a_w0, a_w1, a_w2, a_a0, a_a1, a_a2, a_v0, a_v1, a_v2,
              a_g1, a_g2, a_k_k, a_k_a, a_r_k, a_lnx_g, a_lnx_b, a_w_o,
              b_w_kv, b_w_q, b_w_o, rel_bias,
              moe_w_gc, moe_b_gc, moe_w_gf, moe_b_gf, moe_w_gate, moe_w_up, moe_w_down):
    p = {'ln_g': ln_g, 'ln_b': ln_b, 'a_mu': a_mu, 'a_w_rkv': a_w_rkv, 'a_w0': a_w0, 'a_w1': a_w1,
         'a_w2': a_w2, 'a_a0': a_a0, 'a_a1': a_a1, 'a_a2': a_a2, 'a_v0': a_v0, 'a_v1': a_v1, 'a_v2': a_v2,
         'a_g1': a_g1, 'a_g2': a_g2, 'a_k_k': a_k_k, 'a_k_a': a_k_a, 'a_r_k': a_r_k,
         'a_lnx_g': a_lnx_g, 'a_lnx_b': a_lnx_b, 'a_w_o': a_w_o,
         'b_w_kv': b_w_kv, 'b_w_q': b_w_q, 'b_w_o': b_w_o, 'rel_bias': rel_bias,
         'moe_w_gc': moe_w_gc, 'moe_b_gc': moe_b_gc, 'moe_w_gf': moe_w_gf, 'moe_b_gf': moe_b_gf,
         'moe_w_gate': moe_w_gate, 'moe_w_up': moe_w_up, 'moe_w_down': moe_w_down}
    bp, sp = x_prompt.shape[0], x_prompt.shape[1]
    dt = x_prompt.dtype
    shift0 = jnp.zeros((DEPTH_A, bp, D_MODEL), dt)
    wkv0 = jnp.zeros((DEPTH_A, bp, A_HEADS, A_HEAD, A_HEAD), dt)
    no_past = tuple(jnp.zeros((bp, 0, 2, B_KV_HEADS, B_HEAD), dt) for _ in range(N_GROUPS_B))
    y_prompt, wkv_prompt, shift_prompt, kv_prompt = trunk(x_prompt, shift0, wkv0, no_past, p)
    kv_g0_prompt = kv_prompt[:, sp - min(WINDOWS[0], sp):, 0]
    kv_g1_prompt = kv_prompt[:, sp - min(WINDOWS[1], sp):, 1]
    kv_g2_prompt = kv_prompt[:, sp - min(WINDOWS[2], sp):, 2]
    y_sample, wkv_sample, shift_sample, kv_sample = trunk(
        x_sample, state_a_shift, state_a_wkv, (cache_kv_g0, cache_kv_g1, cache_kv_g2), p)
    return (y_prompt, y_sample, wkv_prompt, shift_prompt, kv_g0_prompt, kv_g1_prompt, kv_g2_prompt,
            wkv_sample, shift_sample, kv_sample[:, :, 0], kv_sample[:, :, 1], kv_sample[:, :, 2])


_drawn_inputs = setup_inputs


def setup_inputs(seed=0):
    import zlib

    import numpy as np

    out = dict(_drawn_inputs(seed))
    spreads = {}
    factors = {'cache_kv_g2': 3.694,
     'a_lnx_g': 4.692,
     'a_lnx_b': 8.0,
     'moe_b_gc': 8.0,
     'moe_b_gf': 25.794,
     'cache_kv_g0': 7.044,
     'cache_kv_g1': 8.0}
    for name, (base, spread) in spreads.items():
        noise = np.random.default_rng([zlib.crc32(name.encode()), seed]).standard_normal(out[name].shape)
        drawn = base * np.exp(spread * noise) if base else spread * noise
        out[name] = jnp.asarray(drawn.astype(out[name].dtype))
    for name, factor in factors.items():
        out[name] = (out[name] * factor).astype(out[name].dtype)
    return out
```

```python
import math
from contextlib import ExitStack

import numpy as np
import concourse.bass as bass
from concourse import mybir

F32 = mybir.dt.float32
I32 = mybir.dt.int32
U32 = mybir.dt.uint32
ACT = mybir.ActivationFunctionType
ALU = mybir.AluOpType
AX = mybir.AxisListType.X

D = 1024
SEQ = 512
REQ = 8
ROWS = SEQ + REQ
TILES = 5
KT = D // 128
HALF = ROWS // 2
HEADS = 16
HD = 64
PAIRS = HEADS // 2
CHUNK = 64
CHUNKS = SEQ // CHUNK
EXPERTS = 16
GROUPS = 4
HIDDEN = 512
ALPHA = 4.0 ** 0.25
LN_EPS = 1e-5
LNX_EPS = 64e-5
KVH = 4
REP = 4
NEG = -1.0e30
DECAY = -math.exp(-0.5)
RING = 6
SLOT = 2048
WORK = (2 * ROWS + EXPERTS * 127) // 128


def tile_rows(t):
    return 128 if t < 4 else REQ


def t5_bucket(dist):
    dist = np.asarray(dist)
    d = np.maximum(dist, 1).astype(np.float32)
    large = 16 + (np.log(d / np.float32(16)) / np.float32(math.log(2048 / 16)) * np.float32(16)).astype(np.int32)
    return np.where(dist < 16, dist, np.minimum(large, 31))


class Layout:

    def __init__(self):
        self.at, self.parts, self.n = {}, [], 0

    def add(self, name, a):
        full = np.zeros((128, a.shape[1]), np.float32)
        full[:a.shape[0]] = a
        self.at[name] = (self.n, a.shape[1])
        self.parts.append(full)
        self.n += a.shape[1]


def bias_rows(offsets, dist):
    out = np.zeros((33, len(offsets)), np.float32)
    for x, (o, ok) in enumerate(offsets):
        if ok:
            out[int(t5_bucket(dist * o)), x] = 1.0
        else:
            out[32, x] = NEG
    return out


def attention_constants():
    c = Layout()
    i = np.arange(128)
    o0 = [(255 - x, 0 <= 255 - x <= 128) for x in range(384)]
    o1 = [(127 - x, 127 - x >= 0) for x in range(160)]
    o2 = [(127 - x, 127 - x >= 0 and (127 - x) % 4 == 0) for x in range(160)]
    c.add("steps", np.concatenate([bias_rows(o0, 1), bias_rows(o1, 4), bias_rows(o2, 4)], 1))
    d0 = [(128 - x, True) for x in range(128)]
    d2 = [(32 - x, True) for x in range(32)]
    own = [(0, True)] * 3
    c.add("decsteps", np.concatenate([bias_rows(d0, 1), bias_rows(d0, 4), bias_rows(d2, 16), bias_rows(own, 1)], 1))
    rq = (i % 32) // 4
    c.add("ownmask", np.tile(np.where(rq[:, None] == np.arange(8)[None], 0.0, NEG).astype(np.float32), (1, 3)))
    return c


def constants():
    c = Layout()
    i = np.arange(128)
    same = (i[:, None] // 64 == i[None, :] // 64).astype(np.float32)
    c.add("ident", np.eye(128, dtype=np.float32))
    c.add("headsum", same)
    c.add("center", np.eye(128, dtype=np.float32) - same / 64)
    for level in range(6):
        size = 1 << level
        m = (i[:, None] // (2 * size) == i[None, :] // (2 * size)) & (i[:, None] // size % 2 == 1) & (i[None, :] // size % 2 == 0)
        c.add(f"level{level}", (m if level == 0 else m.T).astype(np.float32))
    s, t = np.arange(64)[:, None], np.arange(64)[None, :]
    strict, incl = (s < t).astype(np.float32), (s <= t).astype(np.float32)
    even = np.block([[np.zeros((64, 64), np.float32), incl], [strict, incl]])
    odd = np.block([[strict, incl], [np.zeros((64, 64), np.float32), incl]])
    c.add("gmask", np.concatenate([even, odd], 1))
    c.add("first", np.repeat((np.arange(SEQ) % CHUNK != 0).astype(np.float32)[None], 128, 0))
    c.add("ones", np.ones((128, 128), np.float32))
    c.add("earlier", (i[:, None] < i[None, :]).astype(np.float32))
    c.add("rank16", np.repeat(np.arange(16, 0, -1, dtype=np.float32)[None], 128, 0))
    c.add("valid", np.stack([(np.arange(128) < tile_rows(t)) for t in range(TILES)], 1).astype(np.float32))
    c.add("tileno", np.repeat(np.repeat(np.arange(WORK, dtype=np.float32), EXPERTS)[None], 128, 0))
    c.add("pairno", np.repeat(2.0 * np.arange(WORK // 2, dtype=np.float32)[None], 128, 0))
    c.add("rowno", (i[:, None] + 128 * np.arange(TILES)[None]).astype(np.float32))
    return c


class Core:

    def __init__(self, nc, stack, io):
        self.nc, self.io, self.stack = nc, io, stack
        self.names = 0
        self.layout = constants()
        self.banks = [stack.enter_context(nc.psum_tensor(f"bank{i}", [128, 512], F32)) for i in range(8)]
        self.const = self.sb(stack, "const", [128, self.layout.n])
        self.ring = self.sb(stack, "ring", [128, RING, SLOT])
        self.phase = []
        self.landed = [nc.alloc_semaphore(f"weights_landed{i}") for i in range(RING)]
        self.slot_free = nc.alloc_semaphore("weight_slot_free")
        self.table = self.dram("rows", [ROWS, D])
        self.issued = 0
        self.landing = [0] * RING
        self.lands_at = []
        self.used = 0

    def sem(self, name):
        self.names += 1
        self.phase.append(self.nc.alloc_semaphore(f"{name}_{self.names}"))
        return self.phase[-1]

    def next_phase(self):
        self.nc.clear_and_free_semaphores(self.phase)
        self.nc.all_engine_barrier()
        self.phase = []

    def sb(self, stack, name, shape, dt=F32):
        self.names += 1
        return stack.enter_context(self.nc.sbuf_tensor(f"{name}_{self.names}", shape, dt))

    def dram(self, name, shape, dt=F32):
        self.names += 1
        return self.nc.dram_tensor(f"{name}_{self.names}", shape, dt).ap()

    def c(self, name, rows=128):
        at, n = self.layout.at[name]
        return self.const[0:rows, at:at + n]

    def att(self, table, name, rows=128):
        layout, tile = table
        at, n = layout.at[name]
        return tile[0:rows, at:at + n]

    def load_chunk(self, sp, view, src):
        i = self.issued
        if i >= RING:
            sp.wait_ge(self.slot_free, i - RING + 1)
        for v, part in (((view, src),) if callable(view) else zip(view, src)):
            sp.dma_start(v(self.ring[:, i % RING]), part).then_inc(self.landed[i % RING], 16)
            self.landing[i % RING] += 16
        self.lands_at.append(self.landing[i % RING])
        self.issued += 1

    def take_chunk(self, pe):
        i = self.used
        pe.wait_ge(self.landed[i % RING], self.lands_at[i])
        self.used += 1
        return self.ring[:, i % RING]


def columns(w, at, n=256):
    return w.rearrange("(k p) n -> p k n", p=128)[:, :, at:at + n]


def as_k(n):
    return lambda slot: slot[:, 0:8 * n].rearrange("p (k n) -> p k n", k=8)


class Feed:

    def __init__(self, core, chunks):
        self.core, self.chunks, self.first = core, chunks, core.issued

    def upto(self, sp, used_here):
        want = min(self.core.used_at_block + used_here + RING - self.first, len(self.chunks))
        while self.core.issued - self.first < want:
            view, src = self.chunks[self.core.issued - self.first]
            self.core.load_chunk(sp, view, src)


def to_feature_major(core, rows, feats, feed=None, wait=None):
    nc, ps = core.nc, core.banks
    turned, copied = core.sem("turned"), core.sem("turn_copied")
    core.used_at_block = core.used
    with nc.Block() as block:
        @block.sync
        def _(sp):
            if feed:
                feed.upto(sp, 0)

        @block.tensor
        def _(pe):
            for b in range(2 * TILES):
                tile, half = divmod(b, 2)
                n = tile_rows(tile)
                if b >= 8:
                    pe.wait_ge(copied, b - 7)
                for q in range(4):
                    kt = 4 * half + q
                    ins = pe.transpose(ps[b % 8][:, q * 128:q * 128 + n], rows[0:n, tile, kt * 128:(kt + 1) * 128],
                                       core.c("ident")[0:n, 0:n])
                ins.then_inc(turned, 1)

        @block.vector
        def _(dve):
            for b in range(2 * TILES):
                tile, half = divmod(b, 2)
                n = tile_rows(tile)
                dve.wait_ge(turned, b + 1)
                src = ps[b % 8][:, :].rearrange("p (q t) -> p q t", q=4)[:, :, 0:n]
                dve.tensor_copy(feats[:, 4 * half:4 * half + 4, tile * 128:tile * 128 + n], src).then_inc(copied, 1)


def load_inputs(core, xrows, vecs, scope):
    nc, io = core.nc, core.io
    got = core.sem("inputs_landed")
    turned, copied = core.sem("vectors_turned"), core.sem("vectors_copied")
    vrows = core.sb(scope, "vrows", [104, 128])
    with nc.Block() as block:
        @block.sync
        def _(sp):
            sp.dma_start(core.const[:], io["const"]).then_inc(got, 16)
            for t in range(4):
                sp.dma_start(xrows[:, t, :], io["x_prompt"][0, t * 128:(t + 1) * 128, :]).then_inc(got, 16)
            sp.dma_start(xrows[0:REQ, 4, :], io["x_sample"].rearrange("b s d -> (b s) d")).then_inc(got, 16)

        @block.scalar
        def _(act):
            act.dma_start(vrows[0:48, :], io["a_mu"][0].rearrange("c (k p) -> (c k) p", p=128)).then_inc(got, 16)
            at = 48
            for name in ("a_w0", "a_a0", "a_k_k", "a_k_a", "a_r_k", "a_lnx_g", "a_lnx_b"):
                src = io[name][0]
                src = src.rearrange("(k a) b -> k (a b)", a=2) if name == "a_r_k" else src.rearrange("(k p) -> k p", p=128)
                act.dma_start(vrows[at:at + 8, :], src).then_inc(got, 16)
                at += 8

        @block.tensor
        def _(pe):
            pe.wait_ge(got, 16 * 14)
            pe.transpose(core.banks[0][:, 0:104], vrows[:, :], core.c("ident", 104)[:, 0:104]).then_inc(turned, 1)

        @block.vector
        def _(dve):
            dve.wait_ge(turned, 1)
            dve.tensor_copy(vecs[:, :], core.banks[0][:, 0:104]).then_inc(copied, 1)


def time_mix_projections(core, x, vecs, out, feed):
    nc, ps, io = core.nc, core.banks, core.io
    with ExitStack() as own:
        delta = core.sb(own, "delta", [128, KT, ROWS])
        mix = [core.sb(own, f"mix{i}", [128, KT, ROWS]) for i in range(2)]
        room = out["v"][:, :, :].rearrange("p k t -> p (k t)")
        w1 = room[:, 0:512].rearrange("p (k n) -> p k n", k=KT)
        a1 = room[:, 512:1024].rearrange("p (k n) -> p k n", k=KT)
        w2, a2, low = room[0:64, 1024:2048], room[0:64, 2048:3072], room[0:64, 3072:3072 + ROWS]
        shrows = mix[1][0:REQ, 0:2, 0:512]
        small = core.sem("lowrank_weights_landed")
        shift_landed, sh = core.sem("shift_landed"), core.sem("shift_turned")
        dl = core.sem("delta_steps")
        mixed, mix_used = core.sem("mix_ready"), core.sem("mix_used")
        mm, ev = core.sem("product_ready"), core.sem("product_evacuated")
        core.used_at_block = core.used
        order = [(1, "w"), (4, "a"), (0, "r"), (2, "k"), (3, "v")]
        with nc.Block() as block:
            @block.sync
            def _(sp):
                sp.dma_start(w1, io["a_w1"][0].rearrange("(k p) n -> p k n", p=128)).then_inc(small, 16)
                sp.dma_start(w2, io["a_w2"][0]).then_inc(small, 16)
                sp.dma_start(a1, io["a_a1"][0].rearrange("(k p) n -> p k n", p=128)).then_inc(small, 16)
                sp.dma_start(a2, io["a_a2"][0]).then_inc(small, 16)
                sp.dma_start(shrows, io["state_a_shift"][0].rearrange("r (a b) -> r a b", a=2)).then_inc(shift_landed, 16)
                feed.upto(sp, 12)

            @block.vector
            def _(dve):
                dve.tensor_tensor(delta[:, :, 1:SEQ], x[:, :, 0:SEQ - 1], x[:, :, 1:SEQ], ALU.subtract).then_inc(dl, 1)
                dve.tensor_scalar(delta[:, :, 0:1], x[:, :, 0:1], -1.0, None, ALU.mult).then_inc(dl, 1)
                dve.wait_ge(sh, 1)
                dve.tensor_tensor(delta[:, :, SEQ:ROWS], ps[7][:, 0:64].rearrange("p (k r) -> p k r", k=KT),
                                  x[:, :, SEQ:ROWS], ALU.subtract).then_inc(dl, 1)
                dve.wait_ge(dl, 3)
                for n, (c, _) in enumerate(order):
                    if n >= 2:
                        dve.wait_ge(mix_used, n - 1)
                    for kt in range(KT):
                        ins = dve.scalar_tensor_tensor(mix[n % 2][:, kt, :], delta[:, kt, :], vecs[:, c * 8 + kt:c * 8 + kt + 1],
                                                       x[:, kt, :], ALU.mult, ALU.add)
                    ins.then_inc(mixed, 1)

            @block.tensor
            def _(pe):
                job = 0
                pe.wait_ge(shift_landed, 16)
                for kt in range(KT):
                    ins = pe.transpose(ps[7][:, kt * 8:kt * 8 + 8], shrows[:, kt // 4, (kt % 4) * 128:(kt % 4 + 1) * 128],
                                       core.c("ident")[0:REQ, 0:REQ])
                ins.then_inc(sh, 1)
                pe.wait_ge(small, 64)
                pe.wait_ge(dl, 3)
                for n, (c, name) in enumerate(order):
                    pe.wait_ge(mixed, n + 1)
                    m = mix[n % 2]
                    if name in "wa":
                        first, second, lw = (w1, w2, low) if name == "w" else (a1, a2, low)
                        if job >= 4:
                            pe.wait_ge(ev, job - 3)
                        for h in range(2):
                            for kt in range(KT):
                                ins = pe.matmul(ps[2 * (job % 4) + h][0:64, 0:HALF], first[:, kt, :],
                                                m[:, kt, h * HALF:(h + 1) * HALF], start=kt == 0, stop=kt == KT - 1)
                        ins.then_inc(mm, 1)
                        job += 1
                        pe.wait_ge(ev, job)
                        for mt in range(8):
                            if job >= 4:
                                pe.wait_ge(ev, job - 3)
                            for h in range(2):
                                ins = pe.matmul(ps[2 * (job % 4) + h][:, 0:HALF], second[:, mt * 128:(mt + 1) * 128],
                                                lw[:, h * HALF:(h + 1) * HALF], start=True, stop=True)
                            ins.then_inc(mm, 1)
                            job += 1
                        pe.wait_ge(ev, job)
                        pe.drain().then_inc(mix_used, 1)
                        continue
                    for half in range(4):
                        w = as_k(256)(core.take_chunk(pe))
                        for q in range(2):
                            if job >= 4:
                                pe.wait_ge(ev, job - 3)
                            for h in range(2):
                                for kt in range(KT):
                                    ins = pe.matmul(ps[2 * (job % 4) + h][:, 0:HALF], w[:, kt, q * 128:(q + 1) * 128],
                                                    m[:, kt, h * HALF:(h + 1) * HALF], start=kt == 0, stop=kt == KT - 1)
                            ins.then_inc(mm, 1)
                            job += 1
                        pe.drain().then_inc(core.slot_free, 1)
                    pe.drain().then_inc(mix_used, 1)

            @block.scalar
            def _(act):
                job = 0

                def evacuate(dst, func, bias=0.0, rows=128):
                    nonlocal job
                    act.wait_ge(mm, job + 1)
                    for h in range(2):
                        ins = act.activation(dst[0:rows, h * HALF:(h + 1) * HALF], ps[2 * (job % 4) + h][0:rows, 0:HALF], func,
                                             **({} if isinstance(bias, float) else {"bias": bias}))
                    ins.then_inc(ev, 1)
                    job += 1

                for n, (c, name) in enumerate(order):
                    if name in "wa":
                        evacuate(low, ACT.Tanh if name == "w" else ACT.Copy, rows=64)
                        for mt in range(8):
                            b = (48 if name == "w" else 56) + mt
                            evacuate(out[name][:, mt], ACT.Sigmoid, bias=vecs[:, b:b + 1])
                    else:
                        for mt in range(8):
                            evacuate(out[name][:, mt], ACT.Copy)


def time_mix_keys(core, f, vecs, kk, tmp):
    nc, ps = core.nc, core.banks
    step, sq, sm, rt = core.sem("keys_step"), core.sem("square_ready"), core.sem("sum_ready"), core.sem("root_ready")
    core.used_at_block = core.used
    with nc.Block() as block:
        @block.vector
        def _(dve):
            done = 0

            def chain(ins):
                nonlocal done
                ins.then_inc(step, 1)
                done += 1

            for kt in range(KT):
                chain(dve.tensor_scalar(kk[:, kt], f["k"][:, kt], vecs[:, 64 + kt:65 + kt], None, ALU.mult))
            for kt in range(KT):
                dve.wait_ge(sm, kt + 1)
                for h in range(2):
                    chain(dve.tensor_scalar(tmp[:, kt, h * HALF:(h + 1) * HALF], ps[2 * (kt % 4) + h][:, 0:HALF], 1e-24, None, ALU.max))
            for p in range(PAIRS):
                dve.tensor_tensor_scan(f["w"][:, p, 0:SEQ], core.c("first"), f["w"][:, p, 0:SEQ], 0.0, ALU.mult, ALU.add)
            dve.wait_ge(rt, 2 * KT)
            chain(dve.tensor_tensor(kk[:, :, :], kk[:, :, :], tmp[:, :, :], ALU.mult))
            dve.wait_ge(step, done)
            for kt in range(KT):
                chain(dve.tensor_scalar(tmp[:, kt], f["a"][:, kt], -1.0, vecs[:, 72 + kt:73 + kt], ALU.add, ALU.mult))
            dve.wait_ge(step, done)
            chain(dve.scalar_tensor_tensor(f["k"][:, :, :], tmp[:, :, :], 1.0, f["k"][:, :, :], ALU.add, ALU.mult))
            chain(dve.tensor_tensor(f["a"][:, :, :], f["a"][:, :, :], kk[:, :, :], ALU.mult))

        @block.scalar
        def _(act):
            for kt in range(KT):
                act.wait_ge(step, kt + 1)
                act.activation(tmp[:, kt], kk[:, kt], ACT.Square).then_inc(sq, 1)
            for kt in range(KT):
                act.wait_ge(step, KT + 2 * kt + 2)
                act.activation(tmp[:, kt], tmp[:, kt], ACT.Ln).then_inc(rt, 1)
            for kt in range(KT):
                act.wait_ge(rt, KT + kt)
                act.activation(tmp[:, kt], tmp[:, kt], ACT.Exp, scale=-0.5).then_inc(rt, 1)

        @block.tensor
        def _(pe):
            for kt in range(KT):
                pe.wait_ge(sq, kt + 1)
                if kt >= 4:
                    pe.wait_ge(step, KT + 2 * (kt - 4) + 2)
                for h in range(2):
                    ins = pe.matmul(ps[2 * (kt % 4) + h][:, 0:HALF], core.c("headsum"), tmp[:, kt, h * HALF:(h + 1) * HALF],
                                    start=True, stop=True)
                ins.then_inc(sm, 1)


def time_mix_chunks(core, f, kk):
    nc, ps = core.nc, core.banks
    with ExitStack() as own:
        ars = [core.sb(own, f"ar{i}", [128, PAIRS, 2, 64]) for i in range(2)]
        assert core.issued - core.used <= RING - 2
        spare = [core.ring[:, (core.issued + i) % RING] for i in range(2)]
        bks = [spare[0][:, 1024 * i:1024 * i + 1024].rearrange("p (q b s) -> p q b s", q=PAIRS, b=2) for i in range(2)]
        exs = [spare[1][:, 1024 * i:1024 * i + 1024].rearrange("p (e q s) -> p e q s", e=2, q=PAIRS) for i in range(2)]
        G = core.sb(own, "G", [128, HEADS, 128])
        NB = core.sb(own, "NB", [128, PAIRS, 128])
        T = core.sb(own, "T", [128, PAIRS, 128])
        Tt = core.sb(own, "Tt", [128, PAIRS, 128])
        X = core.sb(own, "X", [128, PAIRS, 128])
        vv = Tt[:, :, :].rearrange("p q (e t) -> p q e t", e=2)
        BK = core.sb(own, "BK", [128, PAIRS, 128])
        Z = core.sb(own, "Z", [128, HEADS, 64])
        W = core.sb(own, "W", [128, PAIRS, 64])
        M = core.sb(own, "M", [128, PAIRS, 64])
        S = {n: core.sem(n) for n in (
            "zeroed", "exp_done", "staged", "v_staged", "scores", "score_used", "turned_v", "v_used", "solve_x", "x_masked",
            "solve_d", "tt_new", "t_turned", "t_new", "w_ready", "w_copied", "u_ready", "u_copied", "y_ready",
            "y_copied", "m_ready", "m_new", "m_sum", "bk_copied", "passed")}
        core.used_at_block = core.used
        Zr = Z[:, :, :].rearrange("p (q e) i -> p q e i", e=2)
        HALVES = (slice(0, 64), slice(64, 128))
        G_banks, N_banks, B_banks = (0, 1, 2, 3), (4, 5), (6, 7)
        with nc.Block() as block:
            @block.scalar
            def _(act):
                def exps(c, b):
                    cols = bass.ds(c * CHUNK, CHUNK)
                    act.activation(exs[b][:, 0], f["w"][:, :, cols], ACT.Exp, scale=DECAY).then_inc(S["exp_done"], 1)
                    act.activation(exs[b][:, 1], f["w"][:, :, cols], ACT.Exp, scale=-DECAY).then_inc(S["exp_done"], 1)

                def chunk(c, half, last=False):
                    cols = bass.ds(c * CHUNK, CHUNK)
                    if not last:
                        act.wait_ge(S["m_new"], c + 1)
                        act.sem_inc(S["passed"], 1)
                        exps(c + 1, 1 - half)
                    act.wait_ge(S["scores"], 3 * c + 3)
                    for b in range(2):
                        ins = act.activation(BK[:, 4 * b:4 * b + 4], ps[B_banks[b]][:, :].rearrange("p (q e) -> p q e", q=4), ACT.Copy)
                    ins.then_inc(S["bk_copied"], 1)
                    for level in range(5):
                        for b in range(2):
                            act.wait_ge(S["t_turned"], 10 * c + 2 * level + b + 1)
                            dst = Tt if level == 0 else T
                            bank = (2, 3)[b] if level == 0 else (4, 5)[b]
                            act.activation(dst[:, 4 * b:4 * b + 4], ps[bank][:, :].rearrange("p (q e) -> p q e", q=4),
                                           ACT.Copy).then_inc(S["t_new"], 1)
                    act.wait_ge(S["y_ready"], c + 1)
                    act.sem_inc(S["passed"], 1)
                    act.activation(f["w"][:, :, cols], ps[2][:, :].rearrange("p (q e) -> p q e", q=8), ACT.Copy).then_inc(S["y_copied"], 1)

                act.sem_inc(S["y_copied"], 1)
                exps(0, 0)
                with act.Fori(0, CHUNKS // 2 - 1) as i:
                    chunk(2 * i, 0)
                    chunk(2 * i + 1, 1)
                chunk(CHUNKS - 2, 0)
                chunk(CHUNKS - 1, 1, last=True)

            @block.vector
            def _(dve):
                dve.memset(M[:, :, :], 0.0).then_inc(S["zeroed"], 1)
                dve.memset(Z[:, :, :], 0.0).then_inc(S["zeroed"], 1)
                dve.memset(NB[:, :, :], 0.0).then_inc(S["zeroed"], 1)
                dve.wait_ge(S["zeroed"], 3)
                dve.sem_inc(S["m_new"], 1)
                dve.sem_inc(S["m_sum"], 1)

                def staging(c, h):
                    ar, bk, ex, cols = ars[h], bks[h], exs[h], bass.ds(c * CHUNK, CHUNK)
                    yield dve.tensor_scalar(ar[:, :, 0, 0:1], kk[:, :, bass.ds(c * CHUNK, 1)], -1.0, None, ALU.mult)
                    yield dve.scalar_tensor_tensor(ar[:, :, 0, 1:CHUNK], kk[:, :, bass.ds(c * CHUNK + 1, CHUNK - 1)], -1.0,
                                                   ex[:, 0, :, 0:CHUNK - 1], ALU.mult, ALU.mult)
                    yield dve.tensor_tensor(ar[:, :, 1], f["r"][:, :, cols], ex[:, 0], ALU.mult)
                    for hp, (b, k) in enumerate(((0, 1), (1, 0))):
                        rows = slice(64 * hp, 64 * hp + 64)
                        yield dve.tensor_tensor(bk[rows, :, b], f["a"][rows, :, cols], ex[rows, 1], ALU.mult)
                        yield dve.tensor_tensor(bk[rows, :, k], f["k"][rows, :, cols], ex[rows, 1], ALU.mult)

                def chunk(c, half, last=False):
                    cols, ex = bass.ds(c * CHUNK, CHUNK), exs[half]
                    todo = staging(c + 1, 1 - half) if not last else iter(())

                    def stage_ahead():
                        for ins in todo:
                            ins.then_inc(S["staged"], 1)
                            break

                    dve.tensor_copy(vv[:, :, 0], f["v"][:, :, cols]).then_inc(S["v_staged"], 1)
                    dve.tensor_copy(vv[:, :, 1], f["v"][:, :, cols]).then_inc(S["v_staged"], 1)
                    dve.wait_ge(S["scores"], 3 * c + 1)
                    Gr = G[:, :, :].rearrange("p (q e) s -> p q e s", e=2)
                    gm = core.c("gmask").rearrange("p (e s) -> p e s", e=2)
                    for b in range(4):
                        hp, q = b % 2, b // 2
                        dve.tensor_tensor(Gr[:, 4 * q:4 * q + 4, hp], ps[b][:, :].rearrange("p (q s) -> p q s", q=4),
                                          gm[:, hp:hp + 1, :].to_broadcast([128, 4, 128]), ALU.mult).then_inc(S["score_used"], 1)
                    dve.wait_ge(S["scores"], 3 * c + 2)
                    for hp in range(2):
                        rows = slice(64 * hp, 64 * hp + 64)
                        dve.tensor_copy(NB[rows, :, 64 * hp:64 * hp + 64],
                                        ps[4 + hp][rows, :].rearrange("p (q s) -> p q s", q=8)).then_inc(S["score_used"], 1)
                    wide = lambda name: core.c(name).rearrange("p (o s) -> p o s", o=1).to_broadcast([128, 4, 128])
                    dve.wait_ge(S["score_used"], 10 * c + 6)
                    for b in range(2):
                        quad = slice(4 * b, 4 * b + 4)
                        dve.tensor_tensor(X[:, quad], NB[:, quad], wide("level0"), ALU.mult).then_inc(S["score_used"], 1)
                        dve.wait_ge(S["score_used"], 10 * c + 7 + 2 * b)
                        dve.tensor_tensor(T[:, quad], X[:, quad], wide("ident"), ALU.add).then_inc(S["score_used"], 1)
                    dve.wait_ge(S["turned_v"], c + 1)
                    for b in range(2):
                        src = ps[b][:, :].rearrange("p (q e i) -> p q e i", q=4, e=2)
                        dve.tensor_copy(Zr[64:128, 4 * b:4 * b + 4, 0], src[64:128, :, 0])
                        ins = dve.tensor_copy(Zr[0:64, 4 * b:4 * b + 4, 1], src[0:64, :, 1])
                    ins.then_inc(S["v_used"], 1)
                    if not last:
                        dve.wait_ge(S["exp_done"], 2 * c + 4)
                    for level in range(1, 6):
                        mask = core.c(f"level{level}").rearrange("p (o s) -> p o s", o=1).to_broadcast([128, 4, 128])
                        for b in range(2):
                            quad = slice(4 * b, 4 * b + 4)
                            dve.wait_ge(S["solve_x"], 10 * c + 2 * (level - 1) + b + 1)
                            dve.tensor_tensor(X[:, quad], ps[b][:, :].rearrange("p (q s) -> p q s", q=4), mask,
                                              ALU.mult).then_inc(S["x_masked"], 1)
                        stage_ahead()
                        for b in range(2):
                            quad = slice(4 * b, 4 * b + 4)
                            dve.wait_ge(S["solve_d"], 10 * c + 2 * (level - 1) + b + 1)
                            dve.tensor_tensor(Tt[:, quad], ps[6 + b][:, :].rearrange("p (q s) -> p q s", q=4), Tt[:, quad],
                                              ALU.add).then_inc(S["tt_new"], 1)
                        if level < 5:
                            stage_ahead()
                    for b in range(2):
                        dve.wait_ge(S["w_ready"], 2 * c + b + 1)
                        dve.tensor_copy(W[:, 4 * b:4 * b + 4], ps[(0, 4)[b]][:, 0:256].rearrange("p (q i) -> p q i", q=4)).then_inc(S["w_copied"], 1)
                    for b in range(2):
                        dve.wait_ge(S["u_ready"], 2 * c + b + 1)
                        for hp in range(2):
                            rows = slice(64 * hp, 64 * hp + 64)
                            dve.tensor_copy(Zr[rows, 4 * b:4 * b + 4, hp],
                                            ps[(1, 5)[b]][rows, 0:256].rearrange("p (q i) -> p q i", q=4)).then_inc(S["u_copied"], 1)
                    dve.wait_ge(S["m_ready"], c + 1)
                    dve.tensor_tensor(M[:, :, :], ps[3][:, :].rearrange("p (q i) -> p q i", q=8), M[:, :, :], ALU.add).then_inc(S["m_sum"], 1)
                    dve.wait_ge(S["m_sum"], c + 2)
                    dve.tensor_tensor(M[:, :, :], M[:, :, :], ex[:, 0, :, 63:64].to_broadcast([128, 8, 64]), ALU.mult).then_inc(S["m_new"], 1)
                    dve.wait_ge(S["y_copied"], c + 2)

                dve.wait_ge(S["exp_done"], 2)
                for ins in staging(0, 0):
                    ins.then_inc(S["staged"], 1)
                with dve.Fori(0, CHUNKS // 2 - 1) as i:
                    chunk(2 * i, 0)
                    chunk(2 * i + 1, 1)
                chunk(CHUNKS - 2, 0)
                chunk(CHUNKS - 1, 1, last=True)

            @block.tensor
            def _(pe):
                def chunk(c, half):
                    ar, bk = ars[half], bks[half]
                    pe.wait_ge(S["staged"], 7 * c + 7)
                    for b in G_banks:
                        hp, q = b % 2, b // 2
                        rows = slice(64 * hp, 64 * hp + 64)
                        if b >= 2:
                            pe.wait_ge(S[{2: "y_copied", 3: "m_sum"}[b]], c + 1)
                        for j in range(4):
                            p = 4 * q + j
                            ins = pe.matmul(ps[b][:, j * 128:(j + 1) * 128], bk[rows, p, :, :], ar[rows, p, :, :], start=True, stop=True)
                    ins.then_inc(S["scores"], 1)
                    for hp in range(2):
                        rows = slice(64 * hp, 64 * hp + 64)
                        for p in range(PAIRS):
                            ins = pe.matmul(ps[4 + hp][rows, p * 64:(p + 1) * 64], ar[rows, p, 0, :], bk[rows, p, hp, :],
                                            start=True, stop=True)
                    ins.then_inc(S["scores"], 1)
                    for p in range(PAIRS):
                        ins = pe.transpose(ps[6 + p // 4][:, (p % 4) * 128:(p % 4) * 128 + 128], bk[:, p, :, :], core.c("ident"))
                    ins.then_inc(S["scores"], 1)
                    pe.wait_ge(S["v_staged"], 2 * c + 2)
                    pe.wait_ge(S["score_used"], 10 * c + 2)
                    for p in range(PAIRS):
                        ins = pe.transpose(ps[p // 4][:, (p % 4) * 128:(p % 4) * 128 + 128], vv[:, p, :, :], core.c("ident"))
                    ins.then_inc(S["turned_v"], 1)
                    for b in range(2):
                        pe.wait_ge(S["score_used"], 10 * c + 8 + 2 * b)
                        for j in range(4):
                            ins = pe.transpose(ps[2 + b][:, j * 128:(j + 1) * 128], T[:, 4 * b + j], core.c("ident"))
                        ins.then_inc(S["t_turned"], 1)
                    pe.wait_ge(S["v_used"], c + 1)
                    pe.wait_ge(S["bk_copied"], c + 1)
                    for level in range(1, 6):
                        for b in range(2):
                            if level == 1:
                                pe.wait_ge(S["t_new"], 10 * c + b + 1)
                            else:
                                pe.wait_ge(S["tt_new"], 10 * c + 2 * (level - 2) + b + 1)
                            for j in range(4):
                                ins = pe.matmul(ps[b][:, j * 128:(j + 1) * 128], NB[:, 4 * b + j], Tt[:, 4 * b + j], start=True, stop=True)
                            ins.then_inc(S["solve_x"], 1)
                            if level > 1:
                                for j in range(4):
                                    ins = pe.transpose(ps[4 + b][:, j * 128:(j + 1) * 128], Tt[:, 4 * b + j], core.c("ident"))
                                ins.then_inc(S["t_turned"], 1)
                        for b in range(2):
                            pe.wait_ge(S["x_masked"], 10 * c + 2 * (level - 1) + b + 1)
                            if level > 1:
                                pe.wait_ge(S["t_new"], 10 * c + 2 * (level - 1) + b + 1)
                            for j in range(4):
                                ins = pe.matmul(ps[6 + b][:, j * 128:(j + 1) * 128], T[:, 4 * b + j], X[:, 4 * b + j], start=True, stop=True)
                            ins.then_inc(S["solve_d"], 1)
                    pe.wait_ge(S["x_masked"], 10 * c + 10)
                    pe.wait_ge(S["m_new"], c + 1)
                    pe.sem_inc(S["passed"], 1)
                    for p in range(PAIRS):
                        for hp, rows in enumerate(HALVES):
                            o = ps[(0, 4)[p // 4]][rows, p % 4 * 64:p % 4 * 64 + 64]
                            pe.matmul(o, ar[rows, p, 0, :], M[rows, p], start=True, stop=False)
                            ins = pe.matmul(o, G[:, 2 * p + hp, 0:64], Z[:, 2 * p + hp, :], start=False, stop=True)
                        if p % 4 == 3:
                            ins.then_inc(S["w_ready"], 1)
                    for p in range(PAIRS):
                        for hp in range(2):
                            rows = slice(64 * hp, 64 * hp + 64)
                            pe.matmul(ps[2][rows, p * 64:(p + 1) * 64], M[rows, p], ar[rows, p, 1, :], start=p == 0, stop=False)
                    pe.wait_ge(S["tt_new"], 10 * c + 10)
                    for p in range(PAIRS):
                        if p % 4 == 0:
                            pe.wait_ge(S["w_copied"], 2 * c + p // 4 + 1)
                        ins = pe.matmul(ps[(1, 5)[p // 4]][:, p % 4 * 64:p % 4 * 64 + 64], Tt[:, p], W[:, p], start=True, stop=True)
                        if p % 4 == 3:
                            ins.then_inc(S["u_ready"], 1)
                    for p in range(PAIRS):
                        if p % 4 == 0:
                            pe.wait_ge(S["u_copied"], 4 * c + p // 2 + 2)
                            pe.sem_inc(S["passed"], 1)
                        for hp in range(2):
                            rows = slice(64 * hp, 64 * hp + 64)
                            ins = pe.matmul(ps[2][rows, p * 64:(p + 1) * 64], Z[:, 2 * p + hp, :], G[:, 2 * p + hp, 64:128], start=False, stop=p == PAIRS - 1)
                    ins.then_inc(S["y_ready"], 1)
                    for p in range(PAIRS):
                        for hp in range(2):
                            rows = slice(64 * hp, 64 * hp + 64)
                            o = ps[3][rows, p * 64:(p + 1) * 64]
                            ins = pe.matmul(o, BK[:, p, 64 * hp:64 * hp + 64], Z[:, 2 * p + hp, :], start=True, stop=True)
                    ins.then_inc(S["m_ready"], 1)

                pe.wait_ge(S["zeroed"], 3)
                with pe.Fori(0, CHUNKS // 2) as i:
                    chunk(2 * i, 0)
                    chunk(2 * i + 1, 1)

        done = core.sem("state_turned")
        copied, stored = core.sem("state_copied"), core.sem("state_stored")
        Sout = X[0:64, :, :]
        with nc.Block() as block:
            @block.tensor
            def _(pe):
                for p in range(PAIRS):
                    ins = pe.transpose(ps[p // 4][0:64, (p % 4) * 128:(p % 4) * 128 + 128], M[:, p], core.c("ident"))
                ins.then_inc(done, 1)

            @block.vector
            def _(dve):
                dve.wait_ge(done, 1)
                for b in range(2):
                    ins = dve.tensor_copy(Sout[:, 4 * b:4 * b + 4], ps[b][0:64, :].rearrange("p (q s) -> p q s", q=4))
                    ins.then_inc(copied, 1)

            @block.sync
            def _(sp):
                sp.wait_ge(copied, 2)
                out = core.io["wkv_prompt"][0, 0].rearrange("h i j -> i h j")
                sp.dma_start(out, Sout.rearrange("i q (e j) -> i (q e) j", e=2)).then_inc(stored, 16)
                sp.wait_ge(stored, 16)


def time_mix_requests(core, f, kk):
    nc, ps, io = core.nc, core.banks, core.io
    vec_dram = core.dram("step_vectors", [6, REQ, D])
    y_dram = core.dram("step_out", [REQ, D])
    names = (("r", f["r"]), ("w", f["w"]), ("k", f["k"]), ("v", f["v"]), ("kk", kk), ("b", f["a"]))
    turned, copied, stored = core.sem("step_turned"), core.sem("step_copied"), core.sem("step_vectors_stored")
    core.used_at_block = core.used
    with ExitStack() as own:
        rows = core.sb(own, "step_rows", [REQ, 6, D])
        with nc.Block() as block:
            @block.tensor
            def _(pe):
                for n, (_, src) in enumerate(names):
                    if n >= 4:
                        pe.wait_ge(copied, 2 * (n - 3))
                    for kt in range(KT):
                        b = 2 * (n % 4) + kt // 4
                        ins = pe.transpose(ps[b][0:REQ, (kt % 4) * 128:(kt % 4 + 1) * 128], src[:, kt, SEQ:ROWS], core.c("ident"))
                    ins.then_inc(turned, 1)

            @block.scalar
            def _(act):
                for n, (name, _) in enumerate(names):
                    act.wait_ge(turned, n + 1)
                    for h in range(2):
                        act.activation(rows[:, n, h * 512:(h + 1) * 512], ps[2 * (n % 4) + h][0:REQ, :],
                                       ACT.Exp if name == "w" else ACT.Copy, scale=DECAY if name == "w" else 1.0).then_inc(copied, 1)

            @block.sync
            def _(sp):
                for n in range(6):
                    sp.wait_ge(copied, 2 * n + 2)
                    sp.dma_start(vec_dram[n], rows[:, n, :]).then_inc(stored, 16)
                sp.wait_ge(stored, 96)
    with ExitStack() as own:
        st = core.sb(own, "state", [128, HD, HD])
        tmp = core.sb(own, "state_tmp", [128, HD, HD])
        vec = core.sb(own, "step_vec", [128, 6, HD])
        sa = core.sb(own, "sa", [128, HD])
        yv = core.sb(own, "yv", [128, HD])
        yrows = core.sb(own, "yrows", [REQ, D])
        got, step, out = core.sem("step_landed"), core.sem("step"), core.sem("step_stored")
        back, turned2, copied2 = core.sem("step_y_landed"), core.sem("step_y_turned"), core.sem("step_y_copied")
        over_i = lambda n: vec[:, n:n + 1, :].to_broadcast([128, HD, HD])
        over_j = lambda a: a.rearrange("p (i o) -> p i o", o=1).to_broadcast([128, HD, HD])
        with nc.Block() as block:
            @block.sync
            def _(sp):
                sp.dma_start(st[:, :, :], io["state_a_wkv"][0].rearrange("r h i j -> (r h) i j")).then_inc(got, 16)
                for n in range(6):
                    sp.dma_start(vec[:, n, :], vec_dram[n].rearrange("r (h j) -> (r h) j", h=HEADS)).then_inc(got, 16)
                sp.wait_ge(step, 7)
                sp.dma_start(io["wkv_sample"][0].rearrange("r h i j -> (r h) i j"), st[:, :, :]).then_inc(out, 16)
                sp.wait_ge(step, 9)
                sp.dma_start(y_dram.rearrange("r (h i) -> (r h) i", h=HEADS), yv[:, :]).then_inc(out, 16)
                sp.wait_ge(out, 32)
                sp.dma_start(yrows[:, :], y_dram).then_inc(back, 16)

            @block.vector
            def _(dve):
                dve.wait_ge(got, 16 * 7)
                steps = (
                    lambda: dve.tensor_tensor(tmp[:, :, :], st[:, :, :], over_i(4), ALU.mult),
                    lambda: dve.tensor_reduce(sa[:, :], tmp[:, :, :], AX, ALU.add),
                    lambda: dve.tensor_tensor(st[:, :, :], st[:, :, :], over_i(1), ALU.mult),
                    lambda: dve.tensor_tensor(tmp[:, :, :], over_j(sa[:, :]), over_i(5), ALU.mult),
                    lambda: dve.tensor_tensor(st[:, :, :], st[:, :, :], tmp[:, :, :], ALU.subtract),
                    lambda: dve.tensor_tensor(tmp[:, :, :], over_j(vec[:, 3, :]), over_i(2), ALU.mult),
                    lambda: dve.tensor_tensor(st[:, :, :], st[:, :, :], tmp[:, :, :], ALU.add),
                    lambda: dve.tensor_tensor(tmp[:, :, :], st[:, :, :], over_i(0), ALU.mult),
                    lambda: dve.tensor_reduce(yv[:, :], tmp[:, :, :], AX, ALU.add),
                )
                for n, s in enumerate(steps):
                    s().then_inc(step, 1)
                    dve.wait_ge(step, n + 1)
                dve.wait_ge(turned2, 1)
                dve.tensor_copy(f["w"][:, :, SEQ:ROWS], ps[0][:, 0:64].rearrange("p (k r) -> p k r", k=KT))

            @block.tensor
            def _(pe):
                pe.wait_ge(back, 16)
                for kt in range(KT):
                    ins = pe.transpose(ps[0][:, kt * 8:kt * 8 + 8], yrows[0:REQ, kt * 128:(kt + 1) * 128], core.c("ident")[0:REQ, 0:REQ])
                ins.then_inc(turned2, 1)



def time_mix_gate(core, x, vecs, f, kk):
    nc, ps, io = core.nc, core.banks, core.io
    y, yc, var, r, k, v = f["w"], f["a"], kk, f["r"], f["k"], f["v"]
    core.used_at_block = core.used
    with nc.Block() as block:
        cen, sq, vs, bs = core.sem("centred"), core.sem("squared"), core.sem("variance"), core.sem("bonus_sum")
        d, prod, root = core.sem("gate_dve"), core.sem("rk_product"), core.sem("root")
        pairs = lambda n: (ps[2 * n], ps[2 * n + 1])

        @block.tensor
        def _(pe):
            for kt in range(KT):
                if kt:
                    pe.wait_ge(d, 3 * kt)
                for h in range(2):
                    ins = pe.matmul(pairs(0)[h][:, 0:HALF], core.c("center"), y[:, kt, h * HALF:(h + 1) * HALF], start=True, stop=True)
                ins.then_inc(cen, 1)
                pe.wait_ge(prod, kt + 1)
                for h in range(2):
                    ins = pe.matmul(pairs(2)[h][:, 0:HALF], core.c("headsum"), r[:, kt, h * HALF:(h + 1) * HALF], start=True, stop=True)
                ins.then_inc(bs, 1)
                pe.wait_ge(sq, kt + 1)
                for h in range(2):
                    ins = pe.matmul(pairs(1)[h][:, 0:HALF], core.c("headsum"), var[:, kt, h * HALF:(h + 1) * HALF], start=True, stop=True)
                ins.then_inc(vs, 1)

        @block.scalar
        def _(act):
            for kt in range(KT):
                act.wait_ge(cen, kt + 1)
                for h in range(2):
                    ins = act.activation(var[:, kt, h * HALF:(h + 1) * HALF], pairs(0)[h][:, 0:HALF], ACT.Square)
                ins.then_inc(sq, 1)
            act.wait_ge(d, 3 * KT)
            act.activation(var[:, :, :], var[:, :, :], ACT.Ln).then_inc(root, 1)
            act.wait_ge(root, 1)
            act.activation(var[:, :, :], var[:, :, :], ACT.Exp, scale=-0.5).then_inc(root, 1)

        @block.vector
        def _(dve):
            for kt in range(KT):
                dve.scalar_tensor_tensor(r[:, kt], r[:, kt], vecs[:, 80 + kt:81 + kt], k[:, kt], ALU.mult, ALU.mult).then_inc(prod, 1)
            for kt in range(KT):
                dve.wait_ge(sq, kt + 1)
                for h in range(2):
                    ins = dve.tensor_copy(yc[:, kt, h * HALF:(h + 1) * HALF], pairs(0)[h][:, 0:HALF])
                ins.then_inc(d, 1)
                dve.wait_ge(bs, kt + 1)
                for h in range(2):
                    ins = dve.tensor_tensor(v[:, kt, h * HALF:(h + 1) * HALF], pairs(2)[h][:, 0:HALF], v[:, kt, h * HALF:(h + 1) * HALF], ALU.mult)
                ins.then_inc(d, 1)
                dve.wait_ge(vs, kt + 1)
                for h in range(2):
                    ins = dve.tensor_scalar(var[:, kt, h * HALF:(h + 1) * HALF], pairs(1)[h][:, 0:HALF], 1.0 / HD, LNX_EPS, ALU.mult, ALU.add)
                ins.then_inc(d, 1)
            dve.wait_ge(root, 2)
            dve.tensor_tensor(yc[:, :, :], yc[:, :, :], var[:, :, :], ALU.mult).then_inc(d, 1)
            dve.wait_ge(d, 3 * KT + 1)
            for kt in range(KT):
                dve.tensor_scalar(yc[:, kt], yc[:, kt], vecs[:, 88 + kt:89 + kt], vecs[:, 96 + kt:97 + kt], ALU.mult, ALU.add).then_inc(d, 1)
            dve.wait_ge(d, 3 * KT + 1 + KT)
            dve.tensor_tensor(yc[:, :, :], yc[:, :, :], v[:, :, :], ALU.add).then_inc(d, 1)

    mix, delta = f["r"], kk
    room = f["k"][:, :, :].rearrange("p k t -> p (k t)")
    g1 = room[:, 0:1280].rearrange("p (k n) -> p k n", k=KT)
    g2a, g2b = room[:, 1280:2304], room[0:32, 2304:3328]
    vroom = f["v"][:, :, :].rearrange("p k t -> p (k t)")
    low_a, low_b = vroom[:, 0:ROWS], vroom[0:32, ROWS:2 * ROWS]
    shrows = vroom[0:REQ, 1040:1040 + D]
    small, sh = core.sem("gate_weights_landed"), core.sem("shift_turned")
    d, mixed = core.sem("gate_delta"), core.sem("gate_mixed")
    mm, ev, lw = core.sem("gate_product"), core.sem("gate_used"), core.sem("gate_low")
    with nc.Block() as block:
        @block.sync
        def _(sp):
            sp.dma_start(shrows, io["state_a_shift"][0]).then_inc(small, 16)
            sp.dma_start(g1, io["a_g1"][0].rearrange("(k p) n -> p k n", p=128)).then_inc(small, 16)
            sp.dma_start(g2a, io["a_g2"][0, 0:128]).then_inc(small, 16)
            sp.dma_start(g2b, io["a_g2"][0, 128:160]).then_inc(small, 16)

        @block.vector
        def _(dve):
            dve.tensor_tensor(delta[:, :, 1:SEQ], x[:, :, 0:SEQ - 1], x[:, :, 1:SEQ], ALU.subtract).then_inc(d, 1)
            dve.tensor_scalar(delta[:, :, 0:1], x[:, :, 0:1], -1.0, None, ALU.mult).then_inc(d, 1)
            dve.wait_ge(sh, 1)
            dve.tensor_tensor(delta[:, :, SEQ:ROWS], ps[7][:, 0:64].rearrange("p (k r) -> p k r", k=KT),
                              x[:, :, SEQ:ROWS], ALU.subtract).then_inc(d, 1)
            dve.wait_ge(d, 3)
            for kt in range(KT):
                ins = dve.scalar_tensor_tensor(mix[:, kt, :], delta[:, kt, :], vecs[:, 40 + kt:41 + kt], x[:, kt, :], ALU.mult, ALU.add)
            ins.then_inc(mixed, 1)
            for mt in range(KT):
                dve.wait_ge(mm, mt + 1)
                for h in range(2):
                    cols = slice(h * HALF, (h + 1) * HALF)
                    ins = dve.tensor_tensor(y[:, mt, cols], ps[2 * (mt % 4) + h][:, 0:HALF], yc[:, mt, cols], ALU.mult)
                ins.then_inc(ev, 1)

        @block.scalar
        def _(act):
            act.wait_ge(lw, 1)
            for h in range(2):
                cols = slice(h * HALF, (h + 1) * HALF)
                act.activation(low_a[:, cols], ps[h][:, 0:HALF], ACT.Sigmoid).then_inc(lw, 1)
                act.activation(low_b[:, cols], ps[2 + h][0:32, 0:HALF], ACT.Sigmoid).then_inc(lw, 1)

        @block.tensor
        def _(pe):
            pe.wait_ge(small, 64)
            for kt in range(KT):
                ins = pe.transpose(ps[7][:, kt * 8:kt * 8 + 8], shrows[:, kt * 128:(kt + 1) * 128], core.c("ident")[0:REQ, 0:REQ])
            ins.then_inc(sh, 1)
            pe.wait_ge(mixed, 1)
            for lo, n, b in ((0, 128, 0), (128, 32, 2)):
                for h in range(2):
                    for kt in range(KT):
                        ins = pe.matmul(ps[b + h][0:n, 0:HALF], g1[:, kt, lo:lo + n], mix[:, kt, h * HALF:(h + 1) * HALF],
                                        start=kt == 0, stop=kt == KT - 1)
            ins.then_inc(lw, 1)
            pe.wait_ge(lw, 5)
            for mt in range(KT):
                if mt >= 4:
                    pe.wait_ge(ev, mt - 3)
                for h in range(2):
                    o, cols = ps[2 * (mt % 4) + h][:, 0:HALF], slice(h * HALF, (h + 1) * HALF)
                    pe.matmul(o, g2a[:, mt * 128:(mt + 1) * 128], low_a[:, cols], start=True, stop=False)
                    ins = pe.matmul(o, g2b[:, mt * 128:(mt + 1) * 128], low_b[:, cols], start=False, stop=True)
                ins.then_inc(mm, 1)


def output_rows(core, z, rows, feed):
    nc, ps = core.nc, core.banks
    mm, ev = core.sem("out_product"), core.sem("out_added")
    core.used_at_block = core.used
    with nc.Block() as block:
        @block.sync
        def _(sp):
            feed.upto(sp, 4)

        @block.tensor
        def _(pe):
            job = 0
            for q in range(4):
                w = as_k(256)(core.take_chunk(pe))
                for t in range(TILES):
                    if job >= 8:
                        pe.wait_ge(ev, job - 7)
                    n = tile_rows(t)
                    for kt in range(KT):
                        ins = pe.matmul(ps[job % 8][0:n, 0:256], z[:, kt, t * 128:t * 128 + n], w[:, kt, :], start=kt == 0, stop=kt == KT - 1)
                    ins.then_inc(mm, 1)
                    job += 1
                pe.drain().then_inc(core.slot_free, 1)

        @block.vector
        def _(dve):
            for job in range(4 * TILES):
                q, t = divmod(job, TILES)
                n = tile_rows(t)
                dve.wait_ge(mm, job + 1)
                r = rows[0:n, t, q * 256:(q + 1) * 256]
                dve.scalar_tensor_tensor(r, r, ALPHA, ps[job % 8][0:n, 0:256], ALU.mult, ALU.add).then_inc(ev, 1)


def norm_rows(core, rows, layer, which, stores, combine=None, feed=None):
    nc, io = core.nc, core.io
    with ExitStack() as own:
        gain = core.sb(own, "gain", [128, D])
        shift = core.sb(own, "shift", [128, D])
        stats = core.sb(own, "stats", [128, TILES, 2, 6])
        mv = core.sb(own, "mv", [128, TILES, 4])
        got, st, root, nrm = core.sem("norm_weights"), core.sem("norm_stats"), core.sem("norm_root"), core.sem("normed")
        scaled, final, out = core.sem("norm_scaled"), core.sem("norm_final"), core.sem("norm_stored")
        ag = core.sem("norm_aggregated")
        if combine:
            plan, results = combine
            pair = [core.sb(own, f"pair{t}", [128, 2, D]) for t in range(TILES)]
            gat, sums = [core.sem(f"pair_gathered{t}") for t in range(TILES)], core.sem("combine_sums")
        core.used_at_block = core.used
        with nc.Block() as block:
            @block.scalar
            def _(act):
                act.dma_start(gain[:, :], io["ln_g"][layer, which:which + 1, :].to_broadcast([128, D])).then_inc(got, 16)
                act.dma_start(shift[:, :], io["ln_b"][layer, which:which + 1, :].to_broadcast([128, D])).then_inc(got, 16)
                for t in range(TILES):
                    n = tile_rows(t)
                    act.wait_ge(ag, 2 * t + 2)
                    act.activation(mv[0:n, t, 2:3], mv[0:n, t, 3:4], ACT.Ln).then_inc(root, 1)
                    act.wait_ge(root, 2 * t + 1)
                    act.activation(mv[0:n, t, 2:3], mv[0:n, t, 2:3], ACT.Exp, scale=-0.5).then_inc(root, 1)

            @block.vector
            def _(dve):
                def statistics(t):
                    n = tile_rows(t)
                    if combine:
                        r = rows[0:n, t, :]
                        dve.wait_ge(gat[t], 32)
                        for k in range(2):
                            dve.wait_ge(sums, TILES + 2 * t if k == 0 else TILES + 2 * t + 1)
                            dve.scalar_tensor_tensor(r, pair[t][0:n, k, :], plan["weights"][0:n, k, t:t + 1], r, ALU.mult, ALU.add).then_inc(sums, 1)
                        dve.wait_ge(sums, TILES + 2 * t + 2)
                    for h in range(2):
                        dve.bn_stats(stats[0:n, t, h, :], rows[0:n, t, h * 512:(h + 1) * 512]).then_inc(st, 1)
                    dve.wait_ge(st, 2 * t + 2)
                    dve.bn_aggr(mv[0:n, t, 0:2], stats[0:n, t].rearrange("p a b -> p (a b)")).then_inc(ag, 1)
                    dve.wait_ge(ag, 2 * t + 1)
                    dve.tensor_scalar(mv[0:n, t, 3:4], mv[0:n, t, 1:2], LN_EPS, None, ALU.add).then_inc(ag, 1)

                def normalise(t):
                    n = tile_rows(t)
                    dve.wait_ge(root, 2 * t + 2)
                    dve.tensor_scalar(rows[0:n, t, :], rows[0:n, t, :], mv[0:n, t, 0:1], mv[0:n, t, 2:3],
                                      ALU.subtract, ALU.mult).then_inc(nrm, 1)
                    if t == 0:
                        dve.wait_ge(got, 32)
                    dve.wait_ge(nrm, t + 1)
                    dve.tensor_tensor(rows[0:n, t, :], rows[0:n, t, :], gain[0:n, :], ALU.mult).then_inc(scaled, 1)

                if combine:
                    for t in range(TILES):
                        r = rows[0:tile_rows(t), t, :]
                        dve.tensor_scalar(r, r, ALPHA, None, ALU.mult).then_inc(sums, 1)
                for t in range(TILES + 1):
                    if t < TILES:
                        statistics(t)
                    if t:
                        normalise(t - 1)

            @block.gpsimd
            def _(pool):
                if combine:
                    for t in range(TILES):
                        n = tile_rows(t)
                        for k in range(2):
                            pool.indirect_dma_start(out=pair[t][0:n, k, :], out_offset=None, in_=results,
                                                    in_offset=bass.IndirectOffsetOnAxis(ap=plan["slots"][0:n, k, t:t + 1], axis=0)).then_inc(gat[t], 16)
                pool.wait_ge(got, 32)
                for t in range(TILES):
                    n = tile_rows(t)
                    pool.wait_ge(scaled, t + 1)
                    pool.tensor_tensor(rows[0:n, t, :], rows[0:n, t, :], shift[0:n, :], ALU.add).then_inc(final, 1)

            @block.sync
            def _(sp):
                if feed:
                    sp.wait_ge(gat[TILES - 1], 32)
                    feed.upto(sp, 0)
                count = 0
                for t in range(TILES):
                    sp.wait_ge(final, t + 1)
                    for dst in stores(t):
                        sp.dma_start(dst, rows[0:tile_rows(t), t, :]).then_inc(out, 16)
                        count += 16
                if count:
                    sp.wait_ge(out, count)


def reload_rows(core, rows):
    nc, io = core.nc, core.io
    got = core.sem("rows_landed")
    with nc.Block() as block:
        @block.sync
        def _(sp):
            for t in range(4):
                sp.dma_start(rows[:, t, :], io["x_prompt"][0, t * 128:(t + 1) * 128, :]).then_inc(got, 16)
            sp.dma_start(rows[0:REQ, 4, :], io["x_sample"].rearrange("b s d -> (b s) d")).then_inc(got, 16)
            sp.wait_ge(got, 80)
            sp.dma_start(io["shift_prompt"][0], rows[127:128, 3, :]).then_inc(got, 16)
            sp.dma_start(io["shift_sample"][0], rows[0:REQ, 4, :]).then_inc(got, 16)
            sp.wait_ge(got, 112)


def query_chunk(w, g, a, b):
    views, parts = [], []
    for r in range(2):
        for nb in range(2):
            at = g * D + ((2 * a + nb) * REP + 2 * b + r) * HD
            views.append(lambda slot, lo=128 * r + 64 * nb: slot.rearrange("p (k c) -> p k c", k=8)[:, :, lo:lo + 64])
            parts.append(columns(w, at, HD))
    return views, parts


def route(core, x, layer, plan):
    nc, ps, io = core.nc, core.banks, core.io
    slot_map = core.dram("slot_map", [(WORK) * 128, 1])
    with ExitStack() as own:
        wr = core.sb(own, "router", [128, KT, 20])
        br = core.sb(own, "router_bias", [128, 20])
        L = core.sb(own, "logits", [128, TILES, 20])
        g = core.sb(own, "g", [128, TILES, 4, 4])
        s = core.sb(own, "s", [128, TILES, 8])
        o = core.sb(own, "o", [128, 3, TILES, 16])
        le = core.sb(own, "le", [128, 2, TILES, 16])
        cnt = core.sb(own, "cnt", [128, 4, 16])
        big = core.sb(own, "big", [128, 16, 5])
        ge = core.sb(own, "ge", [128, WORK, 16])
        sf = core.sb(own, "sf", [128, 2, TILES])
        ef = core.sb(own, "ef", [128, WORK])
        pf = core.sb(own, "pf", [128, 2, WORK // 2])
        rowf = core.sb(own, "rowf", [128, TILES])
        zero = core.sb(own, "zero", [WORK, 128])
        mapped = core.sb(own, "mapped", [WORK, 128])
        got, lg, d = core.sem("router_landed"), core.sem("logits"), core.sem("route_dve")
        ex, rk = core.sem("route_exp"), core.sem("ranks")
        zr, zst, scat, mp, mt = core.sem("zeroed"), core.sem("map_zeroed"), core.sem("map_scattered"), core.sem("map_landed"), core.sem("map_turned")
        count = {"n": 0}
        steps = {}

        with nc.Block() as block:
            @block.sync
            def _(sp):
                sp.dma_start(wr[:, :, 0:4], io["moe_w_gc"][layer].rearrange("(k p) g -> p k g", p=128)).then_inc(got, 16)
                sp.dma_start(wr[:, :, 4:20], io["moe_w_gf"][layer].rearrange("(k p) g e -> p k (g e)", p=128)).then_inc(got, 16)
                sp.dma_start(br[:, 0:4], io["moe_b_gc"][layer:layer + 1].to_broadcast([128, 4])).then_inc(got, 16)
                sp.dma_start(br[:, 4:20], io["moe_b_gf"][layer:layer + 1].rearrange("o g e -> o (g e)").to_broadcast([128, 16])).then_inc(got, 16)
                sp.wait_ge(zr, 1)
                sp.dma_start(slot_map.rearrange("(w p) o -> w (p o)", p=128), zero[:, :]).then_inc(zst, 16)
                sp.wait_ge(scat, 16 * 2 * TILES)
                sp.dma_start(mapped[:, :], slot_map.rearrange("(w p) o -> w (p o)", p=128)).then_inc(mp, 16)

            @block.vector
            def _(dve):
                def step(ins, name=None):
                    ins.then_inc(d, 1)
                    count["n"] += 1
                    if name:
                        steps[name] = count["n"]
                    dve.wait_ge(d, count["n"])

                step(dve.memset(L[:, :, :], 0.0))
                dve.wait_ge(got, 64)
                for t in range(TILES):
                    n = tile_rows(t)
                    dve.wait_ge(lg, t + 1)
                    step(dve.tensor_tensor(L[0:n, t, :], ps[t][0:n, 0:20], br[0:n, :], ALU.add))
                Lg = L[:, :, 0:4]
                rank4 = core.c("rank16")[:, 0:4].rearrange("p (o e) -> p o e", o=1).to_broadcast([128, TILES, 4])
                rank16 = core.c("rank16").rearrange("p (o e) -> p o e", o=1).to_broadcast([128, TILES, 16])
                step(dve.tensor_reduce(s[:, :, 0:1], Lg, AX, ALU.max))
                step(dve.tensor_tensor(g[:, :, 1], Lg, s[:, :, 0:1].to_broadcast([128, TILES, 4]), ALU.subtract), "group_logits")
                step(dve.tensor_scalar(g[:, :, 0], g[:, :, 1], 0.0, None, ALU.is_ge))
                step(dve.tensor_tensor(g[:, :, 0], g[:, :, 0], rank4, ALU.mult))
                step(dve.tensor_reduce(s[:, :, 1:2], g[:, :, 0], AX, ALU.max))
                step(dve.tensor_tensor(g[:, :, 0], g[:, :, 0], s[:, :, 1:2].to_broadcast([128, TILES, 4]), ALU.is_equal))
                step(dve.tensor_scalar(g[:, :, 3], g[:, :, 0], -NEG, NEG, ALU.mult, ALU.add))
                for t in range(TILES):
                    e4 = lambda a: a.rearrange("p (g e) -> p g e", g=4)
                    col = lambda a: a.rearrange("p (g o) -> p g o", o=1).to_broadcast([128, 4, 4])
                    step(dve.tensor_tensor(e4(le[:, 0, t]), e4(L[:, t, 4:20]), col(g[:, t, 0]), ALU.mult))
                    step(dve.tensor_tensor(e4(le[:, 0, t]), e4(le[:, 0, t]), col(g[:, t, 3]), ALU.add))
                for k in range(2):
                    m = s[:, :, 2 + k:3 + k]
                    step(dve.tensor_reduce(m, le[:, 0], AX, ALU.max))
                    step(dve.tensor_tensor(o[:, k], le[:, 0], m.to_broadcast([128, TILES, 16]), ALU.is_equal))
                    step(dve.tensor_tensor(o[:, k], o[:, k], rank16, ALU.mult))
                    step(dve.tensor_reduce(s[:, :, 4:5], o[:, k], AX, ALU.max))
                    step(dve.tensor_tensor(o[:, k], o[:, k], s[:, :, 4:5].to_broadcast([128, TILES, 16]), ALU.is_equal))
                    if k == 0:
                        step(dve.scalar_tensor_tensor(le[:, 0], o[:, 0], 3.0 * NEG, le[:, 0], ALU.mult, ALU.add))
                step(dve.tensor_tensor(s[:, :, 5:6], s[:, :, 3:4], s[:, :, 2:3], ALU.subtract), "pair_logit")
                for k in range(2):
                    step(dve.tensor_tensor(o[:, k], o[:, k], core.c("valid").rearrange("p (t o) -> p t o", o=1).to_broadcast([128, TILES, 16]), ALU.mult))
                step(dve.tensor_tensor(o[:, 2], o[:, 0], o[:, 1], ALU.add), "selected")
                dve.wait_ge(ex, 2)
                step(dve.tensor_reduce(s[:, :, 6:7], g[:, :, 2], AX, ALU.add))
                step(dve.tensor_scalar(s[:, :, 5:6], s[:, :, 7:8], 1.0, None, ALU.add))
                step(dve.tensor_tensor(s[:, :, 6:7], s[:, :, 6:7], s[:, :, 5:6], ALU.mult))
                step(dve.reciprocal(s[:, :, 6:7], s[:, :, 6:7]))
                step(dve.tensor_copy(plan["weights"][:, 0, :].rearrange("p (t o) -> p t o", o=1), s[:, :, 6:7]))
                step(dve.tensor_tensor(plan["weights"][:, 1, :].rearrange("p (t o) -> p t o", o=1), s[:, :, 6:7], s[:, :, 7:8], ALU.mult))
                dve.wait_ge(rk, 2)
                step(dve.tensor_copy(cnt[:, 0], ps[5][:, 0:16]))
                for k in range(5):
                    step(dve.tensor_scalar(big[:, :, k], cnt[:, 0], float(128 * k), None, ALU.is_gt))
                step(dve.tensor_reduce(cnt[:, 1], big[:, :, :], AX, ALU.add))
                step(dve.tensor_tensor_scan(cnt[:, 2], core.c("ones")[:, 0:16], cnt[:, 1], 0.0, ALU.mult, ALU.add))
                step(dve.tensor_tensor(cnt[:, 3], cnt[:, 2], cnt[:, 1], ALU.subtract))
                step(dve.tensor_scalar(cnt[:, 3], cnt[:, 3], 128.0, None, ALU.mult))
                for t in range(TILES):
                    step(dve.tensor_tensor(le[:, 0, t], ps[6][:, t * 16:t * 16 + 16], cnt[:, 3], ALU.add))
                for k in range(2):
                    step(dve.tensor_tensor(le[:, 1], le[:, 0], o[:, k], ALU.mult))
                    step(dve.tensor_reduce(sf[:, k], le[:, 1], AX, ALU.add))
                step(dve.tensor_copy(plan["slots"][:, :, :], sf[:, :, :]))
                step(dve.tensor_copy(rowf[:, :], core.c("rowno")), "slots")
                step(dve.tensor_tensor(ge[:, :, :], core.c("tileno").rearrange("p (w e) -> p w e", e=16),
                                       cnt[:, 2:3, :].to_broadcast([128, WORK, 16]), ALU.is_ge))
                step(dve.tensor_reduce(ef[:, :], ge[:, :, :], AX, ALU.add))
                step(dve.tensor_scalar(ef[:, :], ef[:, :], 15.0, None, ALU.min))
                step(dve.tensor_copy(plan["expert"][:, :], ef[:, :]))
                step(dve.tensor_tensor(pf[:, 0], core.c("pairno"), cnt[:, 2, 15:16].to_broadcast([128, WORK // 2]), ALU.is_lt))
                step(dve.tensor_reduce(pf[:, 1, 0:1], pf[:, 0], AX, ALU.add))
                step(dve.tensor_copy(plan["pairs"][:, :], pf[:, 1, 0:1]))
                step(dve.memset(plan["source"][:, :], 0.0))
                dve.wait_ge(mt, 1)
                step(dve.tensor_copy(plan["source"][:, 0:WORK], ps[7][:, 0:WORK]))

            @block.scalar
            def _(act):
                act.wait_ge(d, steps["group_logits"])
                act.activation(g[:, :, 2], g[:, :, 1], ACT.Exp).then_inc(ex, 1)
                act.wait_ge(d, steps["pair_logit"])
                act.activation(s[:, :, 7:8], s[:, :, 5:6], ACT.Exp).then_inc(ex, 1)

            @block.tensor
            def _(pe):
                pe.wait_ge(got, 64)
                for t in range(TILES):
                    n = tile_rows(t)
                    for kt in range(KT):
                        ins = pe.matmul(ps[t][0:n, 0:20], x[:, kt, t * 128:t * 128 + n], wr[:, kt, :], start=kt == 0, stop=kt == KT - 1)
                    ins.then_inc(lg, 1)
                pe.wait_ge(d, steps["selected"])
                for t in range(TILES):
                    out = ps[6][:, t * 16:t * 16 + 16]
                    for u in range(t + 1):
                        ins = pe.matmul(out, core.c("earlier" if u == t else "ones"), o[:, 2, u], start=u == 0, stop=u == t)
                ins.then_inc(rk, 1)
                for u in range(TILES):
                    ins = pe.matmul(ps[5][:, 0:16], core.c("ones"), o[:, 2, u], start=u == 0, stop=u == TILES - 1)
                ins.then_inc(rk, 1)
                pe.wait_ge(mp, 16)
                pe.transpose(ps[7][:, 0:WORK], mapped[:, :], core.c("ident")[0:WORK, 0:WORK]).then_inc(mt, 1)

            @block.gpsimd
            def _(pool):
                pool.memset(zero[:, :], 0.0).then_inc(zr, 1)
                pool.wait_ge(zst, 16)
                pool.wait_ge(d, steps["slots"])
                for t in range(TILES):
                    n = tile_rows(t)
                    for k in range(2):
                        pool.indirect_dma_start(out=slot_map, out_offset=bass.IndirectOffsetOnAxis(ap=plan["slots"][0:n, k, t:t + 1], axis=0),
                                                in_=rowf[0:n, t:t + 1], in_offset=None).then_inc(scat, 16)


def expert_tiles(core, layer, plan, results, feed=None):
    nc, ps, io = core.nc, core.banks, core.io
    with ExitStack() as own:
        xg = [core.sb(own, f"gathered{i}", [128, D]) for i in range(2)]
        idx = [core.sb(own, f"index{i}", [128, 1], I32) for i in range(2)]
        xT = [core.sb(own, f"xT{i}", [128, KT, 128]) for i in range(2)]
        sg = core.sb(own, "sg", [128, HIDDEN])
        hid = core.sb(own, "hid", [128, HIDDEN])
        hT = core.sb(own, "hT", [128, 4, 128])
        yo = [core.sb(own, f"yo{i}", [128, D]) for i in range(2)]
        ix, gat = core.sem("index_copied"), [core.sem(f"gathered{i}") for i in range(2)]
        xt, xc = core.sem("x_turned"), core.sem("x_copied")
        gu, sd, hd, ht, hc = core.sem("gate_up"), core.sem("sigmoid"), core.sem("hidden"), core.sem("hidden_turned"), core.sem("hidden_copied")
        g1, passed, act_passed = core.sem("gated"), core.sem("passed"), core.sem("scalar_passed")
        spare = core.sem("spare_rows_stored")
        yd, yc, ys = core.sem("down"), core.sem("down_copied"), [core.sem(f"down_stored{i}") for i in range(2)]
        landed, slot_free = [core.sem(f"expert_weights_landed{j}") for j in range(RING)], core.sem("expert_slot_free")
        core.used_at_block = core.used
        gate = io["moe_w_gate"][layer].rearrange("e (k p) n -> e p k n", p=128)
        up = io["moe_w_up"][layer].rearrange("e (k p) n -> e p k n", p=128)
        down = io["moe_w_down"][layer].rearrange("e (k p) n -> e p k n", p=128)
        view = lambda slot: slot.rearrange("p (k n) -> p k n", k=4)
        STEPS = WORK // 2
        in_use = lambda engine: engine.value_load(plan["pairs"][0:1, 0:1], min_val=(2 * ROWS + 255) // 256, max_val=STEPS)
        with nc.Block() as block:
            @block.sync
            def _(sp):
                pairs = in_use(sp)
                with sp.Fori(0, STEPS) as i:
                    with sp.If(i < pairs):
                        for b in range(2):
                            e = sp.value_load(plan["expert"][0:1, bass.ds(2 * i + b, 1)], min_val=0, max_val=EXPERTS - 1)
                            pick = lambda w: w[bass.ds(e, 1)].rearrange("o p k n -> (o p) k n")
                            parts = (pick(gate)[:, 0:4], pick(gate)[:, 4:8], pick(up)[:, 0:4], pick(up)[:, 4:8],
                                     pick(down)[:, :, 0:512], pick(down)[:, :, 512:1024])
                            for j, part in enumerate(parts):
                                sp.wait_ge(slot_free, 12 * i + 6 * b + j + 1)
                                sp.dma_start(view(core.ring[:, j]), part).then_inc(landed[j], 16)

            @block.gpsimd
            def _(pool):
                def gather(i, b):
                    pool.tensor_copy(idx[b][:, :], plan["source"][:, bass.ds(2 * i + b, 1)]).then_inc(ix, 1)
                    pool.wait_ge(ix, 2 * i + b + 1)
                    pool.sem_inc(passed, 1)
                    pool.indirect_dma_start(out=xg[b][:, :], out_offset=None, in_=core.table,
                                            in_offset=bass.IndirectOffsetOnAxis(ap=idx[b][:, 0:1], axis=0)).then_inc(gat[b], 16)
                gather(0, 0)
                gather(0, 1)
                pairs = in_use(pool)
                with pool.Fori(0, STEPS) as i:
                    with pool.If(i < pairs):
                        pool.wait_ge(xt, 4 * i + 2)
                        gather(i + 1, 0)
                    with pool.If(i + 1 < pairs):
                        pool.wait_ge(xt, 4 * i + 4)
                        gather(i + 1, 1)

            @block.tensor
            def _(pe):
                def turn(i, b, halves=(0, 1)):
                    pe.wait_ge(gat[b], 16 * i + 16)
                    for half in halves:
                        for q in range(4):
                            kt = 4 * half + q
                            ins = pe.transpose(ps[half][:, q * 128:(q + 1) * 128], xg[b][:, kt * 128:(kt + 1) * 128], core.c("ident"))
                        ins.then_inc(xt, 1)

                def tile(i, b):
                    w = 2 * i + b
                    slots = [core.ring[:, j] for j in range(6)]
                    pe.wait_ge(xc, 2 * w + 2)
                    for m in range(2):
                        for j in range(2):
                            s = 2 * m + j
                            pe.wait_ge(landed[s], 16 * w + 16)
                            for k in range(4):
                                kt = 4 * j + k
                                ins = pe.matmul(ps[2 + m][:, :], xT[b][:, kt, :], view(slots[s])[:, k, :], start=kt == 0, stop=kt == KT - 1)
                            if j == 0:
                                ins.then_inc(slot_free, 1)
                        ins.then_inc(gu, 1)
                        pe.drain().then_inc(slot_free, 1)
                    turn(i if b == 0 else i + 1, 1 - b, (0,))
                    pe.wait_ge(hd, w + 1)
                    for q in range(4):
                        ins = pe.transpose(ps[4][:, q * 128:(q + 1) * 128], hid[:, q * 128:(q + 1) * 128], core.c("ident"))
                    ins.then_inc(ht, 1)
                    turn(i if b == 0 else i + 1, 1 - b, (1,))
                    pe.wait_ge(hc, w + 1)
                    pe.wait_ge(yc, 2 * w + 2)
                    for m in range(2):
                        s = 4 + m
                        pe.wait_ge(landed[s], 16 * w + 16)
                        for k in range(4):
                            ins = pe.matmul(ps[5 + m][:, :], hT[:, k, :], view(slots[s])[:, k, :], start=k == 0, stop=k == 3)
                        ins.then_inc(yd, 1)
                        pe.drain().then_inc(slot_free, 1)

                pe.sem_inc(slot_free, RING)
                turn(0, 0)
                pairs = in_use(pe)
                with pe.Fori(0, STEPS) as i:
                    with pe.If(i < pairs):
                        tile(i, 0)
                        tile(i, 1)

            @block.scalar
            def _(act):
                act.sem_inc(yc, 2)
                for b in range(2):
                    act.sem_inc(ys[b], 16)
                pairs = in_use(act)
                with act.Fori(0, STEPS) as i:
                    with act.If(i < pairs):
                        act.sem_inc(spare, 32)
                    with act.Else():
                        for b in range(2):
                            act.dma_start(results[bass.ds(128 * (2 * i + b), 128), :], core.const[:, 0:D]).then_inc(spare, 16)
                with act.Fori(0, STEPS) as i:
                    with act.If(i < pairs):
                        for b in range(2):
                            w = 2 * i + b
                            act.wait_ge(gu, 2 * w + 1)
                            act.activation(sg[:, :], ps[2][:, :], ACT.Sigmoid).then_inc(sd, 1)
                            for m in range(2):
                                act.wait_ge(yd, 2 * w + m + 1)
                                if m == 0:
                                    act.wait_ge(ys[b], 16 * i + 16)
                                act.activation(yo[b][:, m * 512:(m + 1) * 512], ps[5 + m][:, :], ACT.Copy).then_inc(yc, 1)
                            act.wait_ge(yc, 2 * w + 4)
                            act.dma_start(results[bass.ds(128 * w, 128), :], yo[b][:, :]).then_inc(ys[b], 16)
                act.wait_ge(spare, 32 * STEPS)
                for b in range(2):
                    act.wait_ge(ys[b], 16 * pairs + 16)
                    act.sem_inc(act_passed, 1)

            @block.vector
            def _(dve):
                def take(b, w, halves=(0, 1)):
                    for half in halves:
                        dve.wait_ge(xt, 2 * w + half + 1)
                        dve.tensor_copy(xT[b][:, 4 * half:4 * half + 4], ps[half][:, :].rearrange("p (q t) -> p q t", q=4)).then_inc(xc, 1)

                def tile(i, b):
                    w = 2 * i + b
                    dve.wait_ge(sd, w + 1)
                    dve.tensor_tensor(sg[:, :], sg[:, :], ps[2][:, :], ALU.mult).then_inc(g1, 1)
                    dve.wait_ge(g1, w + 1)
                    dve.wait_ge(gu, 2 * w + 2)
                    dve.tensor_tensor(hid[:, :], sg[:, :], ps[3][:, :], ALU.mult).then_inc(hd, 1)
                    take(1 - b, w + 1, (0,))
                    dve.wait_ge(ht, w + 1)
                    dve.tensor_copy(hT[:, :, :], ps[4][:, :].rearrange("p (q t) -> p q t", q=4)).then_inc(hc, 1)
                    take(1 - b, w + 1, (1,))

                take(0, 0)
                pairs = in_use(dve)
                with dve.Fori(0, STEPS) as i:
                    with dve.If(i < pairs):
                        tile(i, 0)
                        tile(i, 1)


def moe(core, rows, x, layer, stores, next_chunks=None):
    with ExitStack() as own:
        plan = {"slots": core.sb(own, "slots", [128, 2, TILES], I32), "weights": core.sb(own, "weights", [128, 2, TILES]),
                "expert": core.sb(own, "expert", [128, WORK], I32), "source": core.sb(own, "source", [128, WORK + 2]),
                "pairs": core.sb(own, "pairs", [128, 1], I32)}
        results = core.dram("expert_rows", [WORK * 128, D])
        to_feature_major(core, rows, x)
        route(core, x, layer, plan)
        expert_tiles(core, layer, plan, results)
        feed = Feed(core, next_chunks) if next_chunks else None
        norm_rows(core, rows, layer, 1, stores, (plan, results), feed)
    return feed


def shared_kv(core, x, feed, kF, v0, vcl, vnew, bias):
    nc, ps, io = core.nc, core.banks, core.io
    outs = (io["kv_g0_prompt"], io["kv_g1_prompt"], io["kv_g2_prompt"])
    souts = (io["kv_g0_sample"], io["kv_g1_sample"], io["kv_g2_sample"])
    core.used_at_block = core.used
    with ExitStack() as own:
        kv = core.sb(own, "kv", [128, TILES, 1536])
        mm, ev, tr, tc = core.sem("kv_product"), core.sem("kv_copied"), core.sem("k_turned"), core.sem("k_copied")
        st, vl = core.sem("kv_stored"), core.sem("v_landed")
        with nc.Block() as block:
            @block.gpsimd
            def _(pool):
                bias.store(pool)

            @block.sync
            def _(sp):
                feed.upto(sp, 6)
                sp.wait_ge(st, 16 * 12)
                for g in range(2):
                    for c in range(4):
                        src = outs[1 + g][0].rearrange("(i c) s n d -> c i s (n d)", c=4)[c, :, 1, :]
                        sp.dma_start(vcl[:, g, c, :], src).then_inc(vl, 16)
                sp.wait_ge(vl, 128)

            @block.tensor
            def _(pe):
                job = 0
                for q in range(6):
                    w = as_k(256)(core.take_chunk(pe))
                    for t in range(TILES):
                        if job >= 6:
                            pe.wait_ge(ev, job - 5)
                        n = tile_rows(t)
                        for kt in range(KT):
                            ins = pe.matmul(ps[job % 6][0:n, 0:256], x[:, kt, t * 128:t * 128 + n], w[:, kt, :], start=kt == 0, stop=kt == KT - 1)
                        ins.then_inc(mm, 1)
                        job += 1
                    pe.drain().then_inc(core.slot_free, 1)
                job = 0
                for g in range(3):
                    pe.wait_ge(ev, 6 * TILES)
                    for a in range(2):
                        for t in range(TILES):
                            n = tile_rows(t)
                            if job >= 2:
                                pe.wait_ge(tc, job - 1)
                            pe.transpose(ps[6 + job % 2][:, 0:n], kv[0:n, t, g * 512 + a * 128:g * 512 + a * 128 + 128],
                                         core.c("ident")[0:n, 0:n]).then_inc(tr, 1)
                            job += 1

            @block.scalar
            def _(act):
                for job in range(6 * TILES):
                    q, t = divmod(job, TILES)
                    n = tile_rows(t)
                    act.wait_ge(mm, job + 1)
                    act.activation(kv[0:n, t, q * 256:(q + 1) * 256], ps[job % 6][0:n, 0:256], ACT.Copy).then_inc(ev, 1)
                act.wait_ge(ev, 6 * TILES)
                for g in range(3):
                    for t in range(TILES):
                        if g == 0 and t < 3:
                            continue
                        src = kv[0:tile_rows(t), t, g * 512:(g + 1) * 512]
                        if t == 4:
                            dst = souts[g].rearrange("r o s n d -> r (o s n d)")
                        else:
                            at = 0 if g == 0 else t * 128
                            dst = outs[g][0].rearrange("t s n d -> t (s n d)")[at:at + 128, :]
                        act.dma_start(dst, src).then_inc(st, 16)
                act.wait_ge(st, 16 * 12)

            @block.vector
            def _(dve):
                job = 0
                for g in range(3):
                    for a in range(2):
                        for t in range(TILES):
                            n = tile_rows(t)
                            dve.wait_ge(tr, job + 1)
                            dve.tensor_copy(kF[:, g, a, t * 128:t * 128 + n], ps[6 + job % 2][:, 0:n]).then_inc(tc, 1)
                            job += 1
                for t in range(4):
                    dve.tensor_copy(v0[:, t, :], kv[:, t, 256:512])
                dve.tensor_copy(vnew[0:REQ, :, :], kv[0:REQ, 4, :].rearrange("p (g s c) -> p g s c", g=3, s=2)[:, :, 1, :])


def query_projection(core, x, feed, qF):
    nc, ps = core.nc, core.banks
    mm, ev = core.sem("q_product"), core.sem("q_copied")
    core.used_at_block = core.used
    with nc.Block() as block:
        @block.sync
        def _(sp):
            feed.upto(sp, 12)

        @block.tensor
        def _(pe):
            job = 0
            for q in range(12):
                w = core.take_chunk(pe).rearrange("p (k r c) -> p k r c", k=8, r=2)
                for rr in range(2):
                    if job >= 4:
                        pe.wait_ge(ev, job - 3)
                    for h in range(2):
                        for kt in range(KT):
                            ins = pe.matmul(ps[2 * (job % 4) + h][:, 0:HALF], w[:, kt, rr, :],
                                            x[:, kt, h * HALF:(h + 1) * HALF], start=kt == 0, stop=kt == KT - 1)
                    ins.then_inc(mm, 1)
                    job += 1
                pe.drain().then_inc(core.slot_free, 1)

        @block.scalar
        def _(act):
            for job in range(24):
                g, a, r = job // 8, job // 4 % 2, job % 4
                act.wait_ge(mm, job + 1)
                by_class = qF[:, g, a, 0:SEQ * 4].rearrange("p (c i r) -> p c i r", c=4, r=4)[:, :, :, r]
                own_rows = qF[:, g, a, SEQ * 4:].rearrange("p (q r) -> p q r", r=4)[:, :, r]
                first, second = (ps[2 * (job % 4) + h] for h in range(2))
                n = HALF // 4
                act.activation(by_class[:, :, 0:n], first[:, 0:HALF].rearrange("p (i c) -> p c i", c=4), ACT.Copy, scale=HD ** -0.5)
                act.activation(by_class[:, :, n:128], second[:, 0:SEQ - HALF].rearrange("p (i c) -> p c i", c=4), ACT.Copy, scale=HD ** -0.5)
                act.activation(own_rows, second[:, SEQ - HALF:HALF], ACT.Copy, scale=HD ** -0.5).then_inc(ev, 1)


def request_attention(core, own, ac, qF, kF, vnew, rel, z):
    nc, ps, io = core.nc, core.banks, core.io
    caches = (io["cache_kv_g0"], io["cache_kv_g1"], io["cache_kv_g2"])
    nk = (128, 128, 32)
    keys = [core.sb(own, f"keys{i}", [128, REQ, 256]) for i in range(2)]
    values = core.sb(own, "values", [128, 3, REQ, 256])
    KTs = [core.sb(own, f"KT{i}", [128, 4, 128]) for i in range(2)]
    ST = core.sb(own, "ST", [128, 3, 128])
    relr = core.sb(own, "relr", [33, 3, 128])
    B = core.sb(own, "B", [128, 291])
    A = core.sb(own, "A", [128, 312])
    sm = core.sb(own, "sm", [128, 4])
    PT = core.sb(own, "PT", [128, 3, 128])
    PS, o2 = relr[0:REQ, :, :], ST[0:HD, 0, :]
    got = [core.sem(f"cache_landed{g}") for g in range(3)]
    kt_, kc, sc, d, bi = core.sem("cache_turned"), core.sem("cache_k_copied"), core.sem("dec_scores"), core.sem("dec_dve"), core.sem("dec_bias")
    s2, ex, pt, pv, rr = core.sem("dec_turned"), core.sem("dec_exp"), core.sem("dec_probs_turned"), core.sem("dec_out"), core.sem("rel_spread")
    steps = {}
    with nc.Block() as block:
        @block.sync
        def _(sp):
            for g, every in enumerate((1, 4, 16)):
                for r in range(REQ):
                    src = caches[g][r].rearrange("(k e) s n d -> e k (s n d)", e=every)[0]
                    if g == 2 and r == 0:
                        sp.wait_ge(kt_, 4)
                    sp.dma_start(keys[g % 2][0:nk[g], r, :], src[:, 0:256]).then_inc(got[g], 16)
                    sp.dma_start(values[0:nk[g], g, r, :], src[:, 256:512]).then_inc(got[g], 16)

        @block.vector
        def _(dve):
            done = 0

            def step(ins, name=None):
                nonlocal done
                ins.then_inc(d, 1)
                done += 1
                dve.wait_ge(d, done)
                if name:
                    steps[name] = done

            for g in range(3):
                v = relr[:, g, :].rearrange("b (n q r) -> b n q r", n=4, q=REQ)
                for n in range(4):
                    ins = dve.tensor_copy(v[:, n], rel[:, g, 4 * n:4 * n + 4].rearrange("b (o r) -> b o r", o=1).to_broadcast([33, REQ, 4]))
            ins.then_inc(rr, 1)
            for i in range(12):
                g = i // 4
                dve.wait_ge(kt_, i + 1)
                if i >= 2:
                    dve.wait_ge(sc, i - 1)
                src = ps[2 + i % 2][:, :].rearrange("p (q k) -> p q k", q=4)[:, :, 0:nk[g]]
                dve.tensor_copy(KTs[i % 2][:, :, 0:nk[g]], src).then_inc(kc, 1)
            dve.wait_ge(sc, 12)
            STv = ST[:, :, :].rearrange("p g (a e c) -> p g a e c", a=2, e=2)
            for nb in range(2):
                src = ps[nb][:, 0:192].rearrange("p (g a c) -> p g a c", g=3, a=2)
                step(dve.tensor_copy(STv[:, 0:2, :, nb], src[:, 0:2]))
                step(dve.tensor_copy(STv[0:32, 2, :, nb], src[0:32, 2]))
            steps["st"] = done
            dve.wait_ge(bi, 1)
            step(dve.tensor_copy(B[:, :], ps[4][:, 0:291]))
            dve.wait_ge(s2, 1)
            step(dve.tensor_tensor(A[:, 0:288], ps[5][:, 0:288], B[:, 0:288], ALU.add))
            dve.wait_ge(s2, 2)
            step(dve.tensor_tensor(A[:, 288:312], ps[6][:, 0:24], core.att(ac, "ownmask"), ALU.add))
            own_v = A[:, 288:312].rearrange("p (g c) -> p g c", g=3)
            step(dve.tensor_tensor(own_v, own_v, B[:, 288:291].rearrange("p (g o) -> p g o", o=1).to_broadcast([128, 3, 8]), ALU.add))
            step(dve.tensor_reduce(sm[:, 0:1], A[:, :], AX, ALU.max))
            step(dve.tensor_scalar(sm[:, 1:2], sm[:, 0:1], -1.0, None, ALU.mult), "max")
            dve.wait_ge(ex, 1)
            step(dve.reciprocal(sm[:, 3:4], sm[:, 2:3]))
            step(dve.tensor_scalar(A[:, :], A[:, :], sm[:, 3:4], None, ALU.mult), "probs")
            dve.wait_ge(pt, 1)
            step(dve.tensor_copy(PT[:, 0:2], ps[4][:, 0:256].rearrange("p (g c) -> p g c", g=2)))
            step(dve.tensor_copy(PT[0:32, 2], ps[4][0:32, 256:384]))
            step(dve.tensor_copy(PS[:, :, :], ps[5][0:REQ, 0:384].rearrange("p (g c) -> p g c", g=3)), "pt")
            dve.wait_ge(pv, 1)
            step(dve.tensor_copy(o2, ps[7][0:HD, 0:128]))
            a = ps[6][0:HD, 0:128].rearrange("d (n q h l) -> d l n h q", n=4, q=REQ, h=2)
            b = o2.rearrange("d (n q h l) -> d l n h q", n=4, q=REQ, h=2)
            for lo in range(2):
                dst = z[64 * lo:64 * lo + 64, :, SEQ:ROWS].rearrange("d (n h) q -> d n h q", h=2)
                step(dve.tensor_tensor(dst, a[:, lo], b[:, lo], ALU.add))

        @block.scalar
        def _(act):
            act.wait_ge(d, steps["max"])
            act.activation(A[:, :], A[:, :], ACT.Exp, bias=sm[:, 1:2], accum_out=sm[:, 2:3]).then_inc(ex, 1)

        @block.tensor
        def _(pe):
            def turn(i):
                g, r0 = i // 4, 2 * (i % 4)
                pe.wait_ge(got[g], 32 * REQ)
                if i >= 2:
                    pe.wait_ge(kc, i - 1)
                for j in range(4):
                    r, a = r0 + j // 2, j % 2
                    n = nk[g]
                    ins = pe.transpose(ps[2 + i % 2][:, j * 128:j * 128 + n], keys[g % 2][0:n, r, a * 128:(a + 1) * 128], core.c("ident")[0:n, 0:n])
                ins.then_inc(kt_, 1)

            turn(0)
            for i in range(12):
                if i < 11:
                    turn(i + 1)
                pe.wait_ge(kc, i + 1)
                g, r0 = i // 4, 2 * (i % 4)
                for nb in range(2):
                    for j in range(4):
                        r, a = r0 + j // 2, j % 2
                        rows = slice(64 * nb, 64 * nb + 64)
                        at = ((g * 2 + a) * REQ + r) * 4
                        ins = pe.matmul(ps[nb][0:nk[g], at:at + 4], KTs[i % 2][rows, j, 0:nk[g]], qF[rows, g, a, 4 * (SEQ + r):4 * (SEQ + r) + 4], start=True, stop=True)
                ins.then_inc(sc, 1)
            pe.wait_ge(rr, 1)
            dst = core.att(ac, "decsteps", 33)
            for g, (lo, hi) in enumerate(((0, 128), (128, 256), (256, 288))):
                pe.matmul(ps[4][:, lo:hi], relr[:, g, :], dst[:, lo:hi], start=True, stop=True)
                ins = pe.matmul(ps[4][:, 288 + g:289 + g], relr[:, g, :], dst[:, 288 + g:289 + g], start=True, stop=True)
            ins.then_inc(bi, 1)
            pe.wait_ge(d, steps["st"])
            for g in range(3):
                n = nk[g]
                ins = pe.transpose(ps[5][:, 128 * g:128 * g + n], ST[0:n, g, :], core.c("ident")[0:n, 0:n])
            ins.then_inc(s2, 1)
            for nb in range(2):
                for g in range(3):
                    for a in range(2):
                        n = 2 * a + nb
                        rows = slice(64 * nb, 64 * nb + 64)
                        ins = pe.matmul(ps[6][32 * n:32 * n + 32, 8 * g:8 * g + 8], qF[rows, g, a, 4 * SEQ:4 * ROWS],
                                        kF[rows, g, a, SEQ:ROWS], start=True, stop=True, tile_position=(64 * nb, 32 * n))
            ins.then_inc(s2, 1)
            pe.wait_ge(d, steps["probs"])
            for g in range(3):
                pe.transpose(ps[4][0:nk[g], 128 * g:128 * g + 128], A[:, 128 * g:128 * g + nk[g]], core.c("ident"))
            for g in range(3):
                ins = pe.transpose(ps[5][0:REQ, 128 * g:128 * g + 128], A[:, 288 + 8 * g:296 + 8 * g], core.c("ident"))
            ins.then_inc(pt, 1)
            pe.wait_ge(d, steps["pt"])
            for n in range(4):
                for r in range(REQ):
                    at = 32 * n + 4 * r
                    for g in range(3):
                        k = nk[g]
                        pe.matmul(ps[6][0:HD, at:at + 4], values[0:k, g, r, 64 * n:64 * n + 64], PT[0:k, g, at:at + 4],
                                  start=g == 0, stop=g == 2)
            for n in range(4):
                for g in range(3):
                    ins = pe.matmul(ps[7][0:HD, 32 * n:32 * n + 32], vnew[0:REQ, g, 64 * n:64 * n + 64], PS[:, g, 32 * n:32 * n + 32],
                                    start=g == 0, stop=g == 2)
            ins.then_inc(pv, 1)


class BiasTables:

    def __init__(self, core, ac, rel):
        self.core, self.ac, self.rel = core, ac, rel
        self.parts = ((0, 384, 4), (384, 544, 1), (544, 704, 1))
        self.vecs = [core.dram(f"bias_copies{g}", [HEADS, 32, hi - lo + shift]) for g, (lo, hi, shift) in enumerate(self.parts)]
        self.stored = core.sem("bias_stored")

    def place(self, scope):
        self.near = self.core.sb(scope, "near", [128, KVH, 4, 256])
        self.far = self.core.sb(scope, "far", [128, KVH, 4, 256])

    def place_vectors(self, scope):
        self.v = self.core.sb(scope, "bias_vec", [HEADS, 704])

    def products(self, pe, made):
        for g, (lo, hi, _) in enumerate(self.parts):
            ins = pe.matmul(self.core.banks[g][0:HEADS, 0:hi - lo], self.rel[:, g, :], self.core.att(self.ac, "steps", 33)[:, lo:hi],
                            start=True, stop=True)
        ins.then_inc(made, 1)

    def evacuate(self, dve, made):
        dve.wait_ge(made, 1)
        for g, (lo, hi, _) in enumerate(self.parts):
            dve.tensor_copy(self.v[:, lo:hi], self.core.banks[g][0:HEADS, 0:hi - lo])

    def store(self, pool):
        for g, (lo, hi, _) in enumerate(self.parts):
            src = self.v[:, lo:hi].rearrange("h (o x) -> h o x", o=1).to_broadcast([HEADS, 32, hi - lo])
            pool.dma_start(self.vecs[g][:, :, 0:hi - lo], src).then_inc(self.stored, 16)
        pool.wait_ge(self.stored, 48)

    def rows(self, g, n, at, keys):
        length, head = self.parts[g][1] - self.parts[g][0], 32 * self.vecs[g].shape[2]
        return bass.AP(self.vecs[g].tensor, REP * n * head + at, [[length, 32], [head, REP], [1, keys]])

    def load(self, sp, landed):
        for n in range(KVH):
            for c in range(4):
                sp.dma_start(self.near[:, n, c, :], self.rows(0, n, 127 - c, 256)).then_inc(landed[n], 16)
            for j in range(4):
                w = 32 * (j + 1)
                for g in range(2):
                    sp.dma_start(self.far[:, n, j, g * w:(g + 1) * w], self.rows(1 + g, n, 127 - 32 * j, w)).then_inc(landed[n], 16)


def prompt_attention(core, own, qF, kF, v0, vcl, bias, z):
    nc, ps = core.nc, core.banks
    AB = 3
    A = [core.sb(own, f"A{i}", [128, 512]) for i in range(AB)]
    m = core.sb(own, "m", [128, 8, 4])
    PT = [core.sb(own, f"PT{i}", [128, 4, 128]) for i in range(2)]
    S = {k: core.sem(k) for k in ("scores", "biased", "max_ready", "neg", "exps", "recip", "scaled", "turned", "pt_copied", "out_ready", "out_copied")}
    landed = [core.sem(f"bias_landed{n}") for n in range(KVH)]
    near, far = bias.near, bias.far
    tiles = [(n, c, j) for n in range(KVH) for c in range(4) for j in range(4)]
    U = len(tiles)
    lohi = lambda j: (128 if j == 0 else 0, 256 + 64 * (j + 1))
    with nc.Block() as block:
        @block.sync
        def _(sp):
            bias.load(sp, landed)

        @block.tensor
        def _(pe):
            def scores(u):
                n, c, j = tiles[u]
                a, nb = divmod(n, 2)
                rows = slice(64 * nb, 64 * nb + 64)
                lo, _ = lohi(j)
                w = 32 * (j + 1)
                q = lambda g: qF[rows, g, a, 512 * c + 128 * j:512 * c + 128 * j + 128]
                if u >= 3:
                    pe.wait_ge(S["biased"], 2 * (u - 2))
                o = ps[u % 3]
                pe.matmul(o[:, lo:256], q(0), kF[rows, 0, a, 128 * (j - 1) + lo:128 * (j + 1)], start=True, stop=True)
                pe.matmul(o[:, 256:256 + w], q(1), kF[rows, 1, a, c:c + 4 * w:4], start=True, stop=True)
                pe.matmul(o[:, 256 + w:256 + 2 * w], q(2), kF[rows, 2, a, c:c + 4 * w:4], start=True, stop=True).then_inc(S["scores"], 1)

            def turn(u):
                n, c, j = tiles[u]
                w = 32 * (j + 1)
                pe.wait_ge(S["scaled"], u + 1)
                if u >= 2:
                    pe.wait_ge(S["pt_copied"], 2 * (u - 1))
                o, p = ps[3 + u % 2], A[u % AB]
                for k in range(1 if j == 0 else 0, 2):
                    pe.transpose(o[:, k * 128:(k + 1) * 128], p[:, k * 128:(k + 1) * 128], core.c("ident"))
                for k in range(2):
                    ins = pe.transpose(o[0:w, (2 + k) * 128:(3 + k) * 128], p[:, 256 + k * w:256 + (k + 1) * w], core.c("ident"))
                ins.then_inc(S["turned"], 1)

            def out(u):
                n, c, j = tiles[u]
                w = 32 * (j + 1)
                pe.wait_ge(S["pt_copied"], 2 * u + 2)
                if u >= 2:
                    pe.wait_ge(S["out_copied"], 2 * (u - 1))
                o, p, cols = ps[5 + u % 2][0:HD, 0:128], PT[u % 2], slice(64 * n, 64 * n + 64)
                if j:
                    pe.matmul(o, v0[:, j - 1, cols], p[:, 0], start=True, stop=False)
                pe.matmul(o, v0[:, j, cols], p[:, 1], start=j == 0, stop=False)
                pe.matmul(o, vcl[0:w, 0, c, cols], p[0:w, 2], start=False, stop=False)
                pe.matmul(o, vcl[0:w, 1, c, cols], p[0:w, 3], start=False, stop=True).then_inc(S["out_ready"], 1)

            scores(0)
            scores(1)
            for u in range(U + 1):
                if u + 2 < U:
                    scores(u + 2)
                if u < U:
                    turn(u)
                if u >= 1:
                    out(u - 1)

        @block.vector
        def _(dve):
            def soften(u):
                n, c, j = tiles[u]
                lo, hi = lohi(j)
                a = A[u % AB]
                if u % 16 == 0:
                    dve.wait_ge(landed[n], 16 * 12)
                dve.wait_ge(S["scores"], u + 1)
                if u >= AB:
                    dve.wait_ge(S["turned"], u - AB + 1)
                dve.tensor_tensor(a[:, lo:256], ps[u % 3][:, lo:256], near[:, n, c, lo:256], ALU.add).then_inc(S["biased"], 1)
                dve.tensor_tensor(a[:, 256:hi], ps[u % 3][:, 256:hi], far[:, n, j, 0:hi - 256], ALU.add).then_inc(S["biased"], 1)
                dve.wait_ge(S["biased"], 2 * u + 2)
                dve.tensor_reduce(m[:, u % 8, 0:1], a[:, lo:hi], AX, ALU.max).then_inc(S["max_ready"], 1)
                dve.wait_ge(S["max_ready"], u + 1)
                dve.tensor_scalar(m[:, u % 8, 1:2], m[:, u % 8, 0:1], -1.0, None, ALU.mult).then_inc(S["neg"], 1)

            def invert(u):
                dve.wait_ge(S["exps"], u + 1)
                dve.reciprocal(m[:, u % 8, 3:4], m[:, u % 8, 2:3]).then_inc(S["recip"], 1)

            def keep(u):
                n, c, j = tiles[u]
                dve.wait_ge(S["out_ready"], u + 1)
                src = ps[5 + u % 2][0:HD, 0:128].rearrange("d (i h l) -> d l h i", h=2, l=2)
                for lo in range(2):
                    dst = z[64 * lo:64 * lo + 64, 2 * n:2 * n + 2, c + 128 * j:c + 128 * j + 128:4]
                    dve.tensor_copy(dst, src[:, lo]).then_inc(S["out_copied"], 1)

            for u in range(U + 3):
                if u < U:
                    soften(u)
                if 1 <= u <= U:
                    invert(u - 1)
                if u >= 3:
                    keep(u - 3)

        @block.gpsimd
        def _(pool):
            for u in range(U):
                lo, hi = lohi(tiles[u][2])
                a = A[u % AB]
                pool.wait_ge(S["recip"], u + 1)
                pool.tensor_scalar(a[:, lo:hi], a[:, lo:hi], m[:, u % 8, 3:4], 1.0, ALU.mult, ALU.mult).then_inc(S["scaled"], 1)

        @block.scalar
        def _(act):
            def exps(u):
                lo, hi = lohi(tiles[u][2])
                a = A[u % AB]
                act.wait_ge(S["neg"], u + 1)
                act.activation(a[:, lo:hi], a[:, lo:hi], ACT.Exp, bias=m[:, u % 8, 1:2], accum_out=m[:, u % 8, 2:3]).then_inc(S["exps"], 1)

            def copy(u):
                j = tiles[u][2]
                w = 32 * (j + 1)
                k = 1 if j == 0 else 0
                act.wait_ge(S["turned"], u + 1)
                if u >= 2:
                    act.wait_ge(S["out_ready"], u - 1)
                src = ps[3 + u % 2][:, :].rearrange("p (k q) -> p k q", k=4)
                act.activation(PT[u % 2][:, k:2], src[:, k:2], ACT.Copy).then_inc(S["pt_copied"], 1)
                act.activation(PT[u % 2][0:w, 2:4], src[0:w, 2:4], ACT.Copy).then_inc(S["pt_copied"], 1)

            for u in range(U + 2):
                if u < U:
                    exps(u)
                if u >= 2:
                    copy(u - 2)


def rows_from_table(core, scope):
    rows = core.sb(scope, "rows", [128, TILES, D])
    back = core.sem("rows_back")
    with core.nc.Block() as block:
        @block.sync
        def _(sp):
            for t in range(TILES):
                sp.dma_start(rows[0:tile_rows(t), t, :], core.table[t * 128:t * 128 + tile_rows(t), :]).then_inc(back, 16)
            sp.wait_ge(back, 80)
    return rows


def attention(core, x, feed):
    nc, io = core.nc, core.io
    with ExitStack() as s1:
        table = attention_constants()
        ac = (table, core.sb(s1, "att_const", [128, table.n]))
        rel = core.sb(s1, "rel", [33, 3, HEADS])
        qF = core.sb(s1, "qF", [128, 3, 2, ROWS * REP])
        kF = core.sb(s1, "kF", [128, 3, 2, ROWS])
        v0 = core.sb(s1, "v0", [128, 4, 256])
        vcl = core.sb(s1, "vcl", [128, 2, 4, 256])
        vnew = core.sb(s1, "vnew", [REQ, 3, 256])
        bias = BiasTables(core, ac, rel)
        got, one, made = core.sem("attention_constants_landed"), core.sem("one_row"), core.sem("bias_product")
        with ExitStack() as s2:
            bias.place_vectors(s2)
            with nc.Block() as block:
                @block.sync
                def _(sp):
                    sp.dma_start(ac[1][:, :], io["att_const"]).then_inc(got, 16)
                    sp.dma_start(rel[0:32, :, :], io["rel_bias"].rearrange("b (g h) -> b g h", g=3)).then_inc(got, 16)

                @block.tensor
                def _(pe):
                    pe.wait_ge(got, 32)
                    pe.wait_ge(one, 1)
                    bias.products(pe, made)

                @block.vector
                def _(dve):
                    dve.memset(rel[32:33, :, :], 1.0).then_inc(one, 1)
                    bias.evacuate(dve, made)
            shared_kv(core, x, feed, kF, v0, vcl, vnew, bias)
        query_projection(core, x, feed, qF)
        with ExitStack() as s2:
            request_attention(core, s2, ac, qF, kF, vnew, rel, x)
        core.next_phase()
        with ExitStack() as s2:
            bias.place(s2)
            prompt_attention(core, s2, qF, kF, v0, vcl, bias, x)


OUTS = [
    ("y_prompt", (1, SEQ, D)), ("y_sample", (REQ, 1, D)),
    ("wkv_prompt", (1, 1, HEADS, HD, HD)), ("shift_prompt", (1, 1, D)),
    ("kv_g0_prompt", (1, 128, 2, KVH, HD)), ("kv_g1_prompt", (1, SEQ, 2, KVH, HD)), ("kv_g2_prompt", (1, SEQ, 2, KVH, HD)),
    ("wkv_sample", (1, REQ, HEADS, HD, HD)), ("shift_sample", (1, REQ, D)),
    ("kv_g0_sample", (REQ, 1, 2, KVH, HD)), ("kv_g1_sample", (REQ, 1, 2, KVH, HD)), ("kv_g2_sample", (REQ, 1, 2, KVH, HD)),
]


def program(nc, io):
    with ExitStack() as st:
        core = Core(nc, st, io)
        vecs = core.sb(st, "vecs", [128, 104])
        chunks = [(as_k(256), columns(io["a_w_rkv"][0, j], 256 * q)) for j in (0, 1, 2) for q in range(4)]
        chunks += [(as_k(256), columns(io["a_w_o"][0], 256 * q)) for q in range(4)]
        feed = Feed(core, chunks)
        with ExitStack() as s1:
            f = {n: core.sb(s1, n, [128, KT, ROWS]) for n in "rkvaw"}
            with ExitStack() as s2:
                x = core.sb(s2, "x", [128, KT, ROWS])
                with ExitStack() as s3:
                    xrows = core.sb(s3, "xrows", [128, TILES, D])
                    load_inputs(core, xrows, vecs, s3)
                    to_feature_major(core, xrows, x, feed)
                time_mix_projections(core, x, vecs, f, feed)
                core.next_phase()
            with ExitStack() as s2:
                kk = core.sb(s2, "kk", [128, KT, ROWS])
                with ExitStack() as s3:
                    tmp = core.sb(s3, "tmp", [128, KT, ROWS])
                    time_mix_keys(core, f, vecs, kk, tmp)
                time_mix_chunks(core, f, kk)
                core.next_phase()
                time_mix_requests(core, f, kk)
                rows = core.sb(s2, "rows", [128, TILES, D])
                x = core.sb(s2, "x", [128, KT, ROWS])
                reload_rows(core, rows)
                to_feature_major(core, rows, x)
                time_mix_gate(core, x, vecs, f, kk)
                output_rows(core, f["w"], rows, feed)
                norm_rows(core, rows, 0, 0, lambda t: [core.table[t * 128:t * 128 + tile_rows(t), :]])
                core.next_phase()
        kvw = io["b_w_kv"].rearrange("d g s n h -> d (g s n h)")
        chunks = [(as_k(256), columns(kvw, 256 * q)) for q in range(6)]
        chunks += [query_chunk(io["b_w_q"][0], g, a, b) for g in range(3) for a in range(2) for b in range(2)]
        chunks += [(as_k(256), columns(io["b_w_o"][0], 256 * q)) for q in range(4)]
        to_table = lambda t: [core.table[t * 128:t * 128 + tile_rows(t), :]]
        x = core.sb(st, "x", [128, KT, ROWS])
        with ExitStack() as s1:
            rows = rows_from_table(core, s1)
            feed = moe(core, rows, x, 0, to_table, chunks)
            to_feature_major(core, rows, x)
            core.next_phase()
        with ExitStack() as s1:
            attention(core, x, feed)
            rows = rows_from_table(core, s1)
            output_rows(core, x, rows, feed)
            norm_rows(core, rows, 1, 0, to_table)
            core.next_phase()
            yp, ys = io["y_prompt"][0], io["y_sample"].rearrange("r o d -> r (o d)")
            with ExitStack() as s2:
                moe(core, rows, x, 1, lambda t: [yp[t * 128:(t + 1) * 128, :] if t < 4 else ys])
            core.next_phase()


_INS = ["x_prompt", "x_sample", "state_a_wkv", "state_a_shift", "cache_kv_g0", "cache_kv_g1", "cache_kv_g2",
        "ln_g", "ln_b", "a_mu", "a_w_rkv", "a_w0", "a_w1", "a_w2", "a_a0", "a_a1", "a_a2", "a_g1", "a_g2",
        "a_k_k", "a_k_a", "a_r_k", "a_lnx_g", "a_lnx_b", "a_w_o", "b_w_kv", "b_w_q", "b_w_o", "rel_bias",
        "moe_w_gc", "moe_b_gc", "moe_w_gf", "moe_b_gf", "moe_w_gate", "moe_w_up", "moe_w_down"]


def kernel(**inputs):
    import concourse.bacc as _bacc
    from concourse.bass_utils import run_bass_kernel_spmd as _run

    nc = _bacc.Bacc("TRN2", target_bir_lowering=False, num_devices=1)
    arrays, io = {}, {}
    given = {name: np.ascontiguousarray(inputs[name]) for name in _INS}
    given["const"] = np.concatenate(constants().parts, 1)
    given["att_const"] = np.concatenate(attention_constants().parts, 1)
    for name, a in given.items():
        arrays[f"in_{name}"] = a
        io[name] = nc.dram_tensor(f"in_{name}", a.shape, mybir.dt.from_np(a.dtype), kind="ExternalInput").ap()
    for name, shape in OUTS:
        io[name] = nc.dram_tensor(f"out_{name}", shape, F32, kind="ExternalOutput").ap()
    program(nc, io)
    r = _run(nc, [arrays], core_ids=[0])
    return tuple(r.results[0][f"out_{name}"] for name, _ in OUTS)
```
